# Optimizing a Trainium2 kernel written in Bass

```python
import math
import jax, jax.numpy as jnp
from jax import lax
import numpy as np

D_MODEL = 1024
BATCH = 1
SEQ = 128
DEPTH = 2
DEC_BATCH = 1
DEC_SEQ = 512
PAST_LEN = 128

GRID_W = 64
HEAD_DIM = 64
BLOCK = 128
ROPE_THETA = 10000.0
RET_HEADS = 4
RET_WIDTH = RET_HEADS * HEAD_DIM
GQA_HEADS = 4
GQA_KV_HEADS = 2
GQA_WIDTH = GQA_HEADS * HEAD_DIM
SSD_HEADS = 4
SSD_HEAD_DIM = 64
SSD_INNER = SSD_HEADS * SSD_HEAD_DIM
SSD_GROUPS = 2
SSD_STATE = 128
SSD_CONV = 3
SSD_CONV_DIM = SSD_INNER + 2 * SSD_GROUPS * SSD_STATE
SWA_HEADS = 4
SWA_KV_HEADS = 2
SWA_WIDTH = SWA_HEADS * HEAD_DIM
WINDOW = 128
MIX_WIDTH = RET_WIDTH + GQA_WIDTH + SSD_INNER + SWA_WIDTH
D_FF = -(-(8 * D_MODEL) // (3 * 256)) * 256
IN_SPLITS = (RET_WIDTH, RET_WIDTH, RET_WIDTH, RET_WIDTH,
             GQA_WIDTH, GQA_KV_HEADS * HEAD_DIM, GQA_KV_HEADS * HEAD_DIM,
             SSD_INNER, SSD_CONV_DIM, 2 * SSD_HEADS,
             SWA_WIDTH, SWA_KV_HEADS * HEAD_DIM, SWA_KV_HEADS * HEAD_DIM)
IN_WIDTH = sum(IN_SPLITS)
ALPHA = (2.0 * DEPTH) ** 0.25
BETA = (8.0 * DEPTH) ** -0.25

kernel_name = 'hybrid_diffusion_parallel_heads_step'

def layer_norm(x, g, b, eps=1e-5):
    xf = x.astype(jnp.float32)
    mu = jnp.mean(xf, -1, keepdims=True)
    var = jnp.mean(jnp.square(xf - mu), -1, keepdims=True)
    y = (xf - mu) * lax.rsqrt(var + eps) * g.astype(jnp.float32) + b.astype(jnp.float32)
    return y.astype(x.dtype)

def rms_norm(x, g, eps=1e-6):
    xf = x.astype(jnp.float32)
    y = xf * lax.rsqrt(jnp.mean(jnp.square(xf), -1, keepdims=True) + eps) * g.astype(jnp.float32)
    return y.astype(x.dtype)

def head_group_norm(o, g, eps=1e-5):
    mu = jnp.mean(o, -1, keepdims=True)
    var = jnp.mean(jnp.square(o - mu), -1, keepdims=True)
    on = (o - mu) * lax.rsqrt(var + eps)
    return on.reshape(o.shape[:2] + (-1,)) * g.astype(jnp.float32)

def split_columns(p):
    points, acc = [], 0
    for w in IN_SPLITS[:-1]:
        acc += w
        points.append(acc)
    return jnp.split(p, points, axis=-1)

def axial_rope(x):
    L = x.shape[1]
    rows = L // GRID_W
    row = jnp.repeat(jnp.arange(rows, dtype=jnp.float32), GRID_W)
    col = jnp.tile(jnp.arange(GRID_W, dtype=jnp.float32), rows)
    half = x.shape[-1] // 2
    quarter = half // 2
    inv_freq = ROPE_THETA ** (-jnp.arange(quarter, dtype=jnp.float32) / quarter)

    def rotate(xa, pos):
        ang = pos[:, None] * inv_freq[None, :]
        cos = jnp.cos(ang)[None, :, None, :]
        sin = jnp.sin(ang)[None, :, None, :]
        x1, x2 = xa[..., :quarter], xa[..., quarter:]
        return jnp.concatenate([x1 * cos - x2 * sin, x2 * cos + x1 * sin], axis=-1)

    xf = x.astype(jnp.float32)
    out = jnp.concatenate([rotate(xf[..., :half], row), rotate(xf[..., half:], col)], axis=-1)
    return out.astype(x.dtype)

def sink_softmax(s, sink):
    col = jnp.broadcast_to(sink.astype(jnp.float32)[:, :, None, None], s.shape[:-1] + (1,))
    return jax.nn.softmax(jnp.concatenate([s, col], axis=-1), axis=-1)[..., :-1]

def blocked_attention(q, k, v, sink=None):
    bsz, L, hq, hd = q.shape
    hkv = k.shape[2]
    grp = hq // hkv
    nb = L // BLOCK
    qb = jnp.moveaxis(q.reshape(bsz, nb, BLOCK, hkv, grp, hd), 1, 0)

    def one_block(qblk):
        s = jnp.einsum('bqkgd,bskd->bkgqs', qblk, k).astype(jnp.float32) * hd ** -0.5
        p = jax.nn.softmax(s, axis=-1) if sink is None else sink_softmax(s, sink.reshape(hkv, grp))
        return jnp.einsum('bkgqs,bskd->bqkgd', p.astype(v.dtype), v)

    out = lax.map(one_block, qb)
    return jnp.moveaxis(out, 0, 1).reshape(bsz, L, hq, hd)

def banded_attention(q, k, v, kc, vc, sink):
    bsz, N, hq, hd = q.shape
    hkv = k.shape[2]
    grp = hq // hkv
    nb = N // BLOCK
    qb = q.reshape(bsz, nb, BLOCK, hkv, grp, hd)

    def band(a):
        ap = jnp.pad(a, ((0, 0), (BLOCK, BLOCK), (0, 0), (0, 0))).reshape(bsz, nb + 2, BLOCK, hkv, hd)
        return jnp.concatenate([ap[:, :-2], ap[:, 1:-1], ap[:, 2:]], axis=2)

    kb, vb = band(k), band(v)
    qi = jnp.arange(nb)[:, None] * BLOCK + jnp.arange(BLOCK)[None, :]
    kj = (jnp.arange(nb)[:, None] - 1) * BLOCK + jnp.arange(3 * BLOCK)[None, :]
    mask = ((jnp.abs(qi[:, :, None] - kj[:, None, :]) <= WINDOW)
            & (kj[:, None, :] >= 0) & (kj[:, None, :] < N))
    scale = hd ** -0.5
    s_loc = jnp.einsum('bnqkgd,bnskd->bnkgqs', qb, kb).astype(jnp.float32) * scale
    s_loc = jnp.where(mask[None, :, None, None], s_loc, -jnp.inf)
    s_ctx = jnp.einsum('bnqkgd,bskd->bnkgqs', qb, kc).astype(jnp.float32) * scale
    p = sink_softmax(jnp.concatenate([s_loc, s_ctx], axis=-1), sink.reshape(hkv, grp))
    p_loc, p_ctx = p[..., :3 * BLOCK], p[..., 3 * BLOCK:]
    out = (jnp.einsum('bnkgqs,bnskd->bnqkgd', p_loc.astype(v.dtype), vb)
           + jnp.einsum('bnkgqs,bskd->bnqkgd', p_ctx.astype(vc.dtype), vc))
    return out.reshape(bsz, N, hq, hd)

def retention_scan(q, k, v, log_gamma, s0):
    bsz, L, H, _ = q.shape
    dv = v.shape[-1]
    nc = L // BLOCK
    pos = jnp.arange(BLOCK, dtype=jnp.float32)
    diff = pos[:, None] - pos[None, :]
    decay = jnp.exp(jnp.where(diff[None] >= 0, diff[None] * log_gamma[:, None, None], -jnp.inf))
    q_decay = jnp.exp((pos[:, None] + 1.0) * log_gamma[None, :])
    k_decay = jnp.exp((BLOCK - 1.0 - pos[:, None]) * log_gamma[None, :])
    chunk_decay = jnp.exp(BLOCK * log_gamma)

    def to_chunks(a):
        return jnp.moveaxis(a.reshape((bsz, nc, BLOCK) + a.shape[2:]), 1, 0)

    def step(state, blk):
        qc, kc, vc = blk
        attn = jnp.einsum('bqhd,bkhd->bhqk', qc, kc) * decay
        out = (jnp.einsum('bhqk,bkhe->bqhe', attn, vc)
               + jnp.einsum('bqhd,bhde->bqhe', qc, state) * q_decay[None, :, :, None])
        state = (state * chunk_decay[None, :, None, None]
                 + jnp.einsum('bkhd,bkhe->bhde', kc * k_decay[None, :, :, None], vc))
        return state, out

    state, out = lax.scan(step, s0, (to_chunks(q), to_chunks(k), to_chunks(v)))
    return jnp.moveaxis(out, 0, 1).reshape(bsz, L, H, dv), state

def ssd_scan(x, dt, a, bm, cm, h0):
    bsz, L, H, P = x.shape
    nc = L // BLOCK
    lower = jnp.tril(jnp.ones((BLOCK, BLOCK), dtype=bool))

    def to_chunks(t):
        return jnp.moveaxis(t.reshape((bsz, nc, BLOCK) + t.shape[2:]), 1, 0)

    def step(h, blk):
        xc, dtc, bc, cc = blk
        cum = jnp.cumsum(dtc * a, axis=1)
        seg = jnp.exp(jnp.where(lower[None, :, :, None],
                                cum[:, :, None, :] - cum[:, None, :, :], -jnp.inf))
        xdt = xc * dtc[..., None]
        scores = jnp.einsum('bqhn,bkhn->bqkh', cc, bc) * seg
        y = (jnp.einsum('bqkh,bkhp->bqhp', scores, xdt)
             + jnp.einsum('bqhn,bhpn->bqhp', cc, h) * jnp.exp(cum)[..., None])
        to_end = jnp.exp(cum[:, -1:, :] - cum)
        h = (h * jnp.exp(cum[:, -1])[:, :, None, None]
             + jnp.einsum('bkhn,bkhp->bhpn', bc * to_end[..., None], xdt))
        return h, y

    h, y = lax.scan(step, h0, (to_chunks(x), to_chunks(dt), to_chunks(bm), to_chunks(cm)))
    return jnp.moveaxis(y, 0, 1).reshape(bsz, L, H, P), h

def centred_depthwise_conv(x, w, b):
    width, ch = w.shape
    y = lax.conv_general_dilated(x, w[:, None, :], window_strides=(1,),
                                 padding=[((width - 1) // 2, width // 2)],
                                 dimension_numbers=('NWC', 'WIO', 'NWC'), feature_group_count=ch)
    return y + b

def token_mixers(h, lp, ctx):
    f32 = jnp.float32
    bsz, L, _ = h.shape
    latent = ctx is not None
    (rq, rk, rv, rg, gq, gk, gv, sz, sxbc, sdt, wq, wk, wv) = split_columns(h @ lp['w_in'])

    def heads(t, n):
        return t.reshape(bsz, L, n, -1)

    def flip(t):
        return jnp.flip(t, axis=1)

    q_r = heads(rq, RET_HEADS).astype(f32)
    k_r = heads(rk, RET_HEADS).astype(f32) * HEAD_DIM ** -0.5
    v_r = heads(rv, RET_HEADS).astype(f32)
    log_gamma = jnp.log1p(-jnp.exp(lp['ret_decay'].astype(f32)))
    r0 = ctx['ret'].astype(f32) if latent else jnp.zeros((bsz, 2, RET_HEADS, HEAD_DIM, HEAD_DIM), f32)
    o_f, s_f = retention_scan(q_r, k_r, v_r, log_gamma[0], r0[:, 0])
    o_b, s_b = retention_scan(flip(q_r), flip(k_r), flip(v_r), log_gamma[1], r0[:, 1])
    y_ret = (head_group_norm(o_f + flip(o_b), lp['ret_gn_g'])
             * jax.nn.silu(rg.astype(f32))).astype(h.dtype)

    q_g = rms_norm(heads(gq, GQA_HEADS), lp['gqa_q_norm'])
    k_g = rms_norm(heads(gk, GQA_KV_HEADS), lp['gqa_k_norm'])
    v_g = heads(gv, GQA_KV_HEADS)
    if latent:
        y_gqa = blocked_attention(axial_rope(q_g),
                                  jnp.concatenate([axial_rope(k_g), ctx['gqa_k']], axis=1),
                                  jnp.concatenate([v_g, ctx['gqa_v']], axis=1))
    else:
        y_gqa = blocked_attention(q_g, k_g, v_g)
    y_gqa = y_gqa.reshape(bsz, L, GQA_WIDTH)

    xbc = jax.nn.silu(centred_depthwise_conv(sxbc, lp['ssd_conv_w'], lp['ssd_conv_b']))
    xs_, bs_, cs_ = jnp.split(xbc, [SSD_INNER, SSD_INNER + SSD_GROUPS * SSD_STATE], axis=-1)
    rep = SSD_HEADS // SSD_GROUPS
    x_s = xs_.reshape(bsz, L, SSD_HEADS, SSD_HEAD_DIM).astype(f32)
    b_s = jnp.repeat(bs_.reshape(bsz, L, SSD_GROUPS, SSD_STATE), rep, axis=2).astype(f32)
    c_s = jnp.repeat(cs_.reshape(bsz, L, SSD_GROUPS, SSD_STATE), rep, axis=2).astype(f32)
    dt = jax.nn.softplus(sdt.reshape(bsz, L, 2, SSD_HEADS).astype(f32) + lp['ssd_dt_bias'].astype(f32))
    a = -jnp.exp(lp['ssd_a_log'].astype(f32))
    h0 = ctx['ssd'].astype(f32) if latent else jnp.zeros((bsz, 2, SSD_HEADS, SSD_HEAD_DIM, SSD_STATE), f32)
    y_f, h_f = ssd_scan(x_s, dt[:, :, 0], a[0], b_s, c_s, h0[:, 0])
    y_b, h_b = ssd_scan(flip(x_s), flip(dt[:, :, 1]), a[1], flip(b_s), flip(c_s), h0[:, 1])
    y_s = y_f + flip(y_b) + x_s * lp['ssd_d'].astype(f32)[:, None]
    y_s = y_s.reshape(bsz, L, SSD_INNER) * jax.nn.silu(sz.astype(f32))
    y_ssd = rms_norm(y_s, lp['ssd_norm_g']).astype(h.dtype)

    q_w = heads(wq, SWA_HEADS)
    k_w = heads(wk, SWA_KV_HEADS)
    v_w = heads(wv, SWA_KV_HEADS)
    if latent:
        y_swa = banded_attention(axial_rope(q_w), axial_rope(k_w), v_w,
                                 ctx['swa_k'], ctx['swa_v'], lp['swa_sink'])
    else:
        y_swa = blocked_attention(q_w, k_w, v_w, lp['swa_sink'])
    y_swa = y_swa.reshape(bsz, L, SWA_WIDTH)

    out = jnp.concatenate([y_ret, y_gqa, y_ssd, y_swa], axis=-1) @ lp['w_out']
    if latent:
        return out, None
    ret_state = jnp.stack([s_f, s_b], axis=1).astype(h.dtype)
    ssd_state = jnp.stack([h_f, h_b], axis=1).astype(h.dtype)
    return out, (k_g, v_g, k_w, v_w, ret_state, ssd_state)

def swiglu(h, w_in, w_out):
    gate, up = jnp.split(h @ w_in, 2, axis=-1)
    return (jax.nn.silu(gate) * up) @ w_out

def trunk_layer(x, cond, lp, ctx):
    mod = (jax.nn.silu(cond) @ lp['ada_w'] + lp['ada_b'])[:, None, :]
    shift1, scale1, gate1, shift2, scale2, gate2 = jnp.split(mod, 6, axis=-1)
    mix, ctx_out = token_mixers(x * (1 + scale1) + shift1, lp, ctx)
    x = layer_norm(ALPHA * x + gate1 * mix, lp['ln1_g'], lp['ln1_b'])
    ffn = swiglu(x * (1 + scale2) + shift2, lp['w_ffn_in'], lp['w_ffn_out'])
    x = layer_norm(ALPHA * x + gate2 * ffn, lp['ln2_g'], lp['ln2_b'])
    return x, ctx_out

def setup_inputs(seed: int = 0) -> dict:
    key = jax.random.key(seed)
    keys = iter(jax.random.split(key, 48))

    def normal(shape, scale=1.0):
        return scale * jax.random.normal(next(keys), shape, jnp.float32)

    def gain(shape):
        return 1.0 + normal(shape, 0.02)

    gqa_cache = (DEC_BATCH, DEPTH, PAST_LEN, GQA_KV_HEADS, HEAD_DIM)
    swa_cache = (DEC_BATCH, DEPTH, PAST_LEN, SWA_KV_HEADS, HEAD_DIM)
    head_idx = jnp.arange(RET_HEADS, dtype=jnp.float32)
    dir_offset = jnp.array([0.0, 0.5], jnp.float32)
    ret_decay = (-(5.0 + head_idx[None, None, :] + dir_offset[None, :, None]) * math.log(2.0)
                 + normal((DEPTH, 2, RET_HEADS), 0.01))
    dt0 = jnp.exp(jax.random.uniform(next(keys), (DEPTH, 2, SSD_HEADS), jnp.float32,
                                     math.log(1e-3), math.log(1e-1)))
    ssd_dt_bias = dt0 + jnp.log(-jnp.expm1(-dt0))
    ssd_a_log = jnp.log(jax.random.uniform(next(keys), (DEPTH, 2, SSD_HEADS), jnp.float32, 1.0, 16.0))
    return {
        'x_prompt': normal((BATCH, SEQ, D_MODEL)),
        'x_sample': normal((DEC_BATCH, DEC_SEQ, D_MODEL)),
        'cache_gqa_k': normal(gqa_cache),
        'cache_gqa_v': normal(gqa_cache),
        'cache_swa_k': normal(swa_cache),
        'cache_swa_v': normal(swa_cache),
        'state_ret': normal((DEC_BATCH, DEPTH, 2, RET_HEADS, HEAD_DIM, HEAD_DIM), 0.5),
        'state_ssd': normal((DEC_BATCH, DEPTH, 2, SSD_HEADS, SSD_HEAD_DIM, SSD_STATE), 0.5),
        'c': normal((DEC_BATCH, D_MODEL)),
        'c_ctx': normal((D_MODEL,)),
        'ada_w': normal((DEPTH, D_MODEL, 6 * D_MODEL), 0.5 * D_MODEL ** -0.5),
        'ada_b': normal((DEPTH, 6 * D_MODEL), 0.02),
        'w_in': normal((DEPTH, D_MODEL, IN_WIDTH), D_MODEL ** -0.5),
        'ret_decay': ret_decay,
        'ret_gn_g': gain((DEPTH, RET_WIDTH)),
        'gqa_q_norm': gain((DEPTH, HEAD_DIM)),
        'gqa_k_norm': gain((DEPTH, HEAD_DIM)),
        'ssd_conv_w': normal((DEPTH, SSD_CONV, SSD_CONV_DIM), SSD_CONV ** -0.5),
        'ssd_conv_b': normal((DEPTH, SSD_CONV_DIM), 0.02),
        'ssd_dt_bias': ssd_dt_bias,
        'ssd_a_log': ssd_a_log,
        'ssd_d': gain((DEPTH, SSD_HEADS)),
        'ssd_norm_g': gain((DEPTH, SSD_INNER)),
        'swa_sink': normal((DEPTH, SWA_HEADS), 0.5),
        'w_out': normal((DEPTH, MIX_WIDTH, D_MODEL), BETA * MIX_WIDTH ** -0.5),
        'ln1_g': gain((DEPTH, D_MODEL)),
        'ln1_b': normal((DEPTH, D_MODEL), 0.02),
        'w_ffn_in': normal((DEPTH, D_MODEL, 2 * D_FF), D_MODEL ** -0.5),
        'w_ffn_out': normal((DEPTH, D_FF, D_MODEL), BETA * D_FF ** -0.5),
        'ln2_g': gain((DEPTH, D_MODEL)),
        'ln2_b': normal((DEPTH, D_MODEL), 0.02),
    }

def reference(x_prompt, x_sample, cache_gqa_k, cache_gqa_v, cache_swa_k, cache_swa_v, state_ret, state_ssd,
              c, c_ctx, ada_w, ada_b, w_in, ret_decay, ret_gn_g, gqa_q_norm, gqa_k_norm,
              ssd_conv_w, ssd_conv_b, ssd_dt_bias, ssd_a_log, ssd_d, ssd_norm_g, swa_sink, w_out,
              ln1_g, ln1_b, w_ffn_in, w_ffn_out, ln2_g, ln2_b):
    def layer_params(l):
        return {'ada_w': ada_w[l], 'ada_b': ada_b[l], 'w_in': w_in[l], 'ret_decay': ret_decay[l],
                'ret_gn_g': ret_gn_g[l], 'gqa_q_norm': gqa_q_norm[l], 'gqa_k_norm': gqa_k_norm[l],
                'ssd_conv_w': ssd_conv_w[l], 'ssd_conv_b': ssd_conv_b[l], 'ssd_dt_bias': ssd_dt_bias[l],
                'ssd_a_log': ssd_a_log[l], 'ssd_d': ssd_d[l], 'ssd_norm_g': ssd_norm_g[l],
                'swa_sink': swa_sink[l], 'w_out': w_out[l], 'ln1_g': ln1_g[l], 'ln1_b': ln1_b[l],
                'w_ffn_in': w_ffn_in[l], 'w_ffn_out': w_ffn_out[l], 'ln2_g': ln2_g[l], 'ln2_b': ln2_b[l]}

    xp = x_prompt
    cond_ctx = c_ctx[None, :]
    gk_l, gv_l, wk_l, wv_l, rs_l, ss_l = [], [], [], [], [], []
    for l in range(DEPTH):
        xp, (k_g, v_g, k_w, v_w, r_s, s_s) = trunk_layer(xp, cond_ctx, layer_params(l), None)
        gk_l.append(k_g)
        gv_l.append(v_g)
        wk_l.append(k_w)
        wv_l.append(v_w)
        rs_l.append(r_s)
        ss_l.append(s_s)
    new_gqa_k = jnp.stack(gk_l, axis=1)
    new_gqa_v = jnp.stack(gv_l, axis=1)
    new_swa_k = jnp.stack(wk_l, axis=1)
    new_swa_v = jnp.stack(wv_l, axis=1)
    new_state_ret = jnp.stack(rs_l, axis=1)
    new_state_ssd = jnp.stack(ss_l, axis=1)

    xs = x_sample
    for l in range(DEPTH):
        ctx = {'gqa_k': cache_gqa_k[:, l], 'gqa_v': cache_gqa_v[:, l],
               'swa_k': cache_swa_k[:, l], 'swa_v': cache_swa_v[:, l],
               'ret': state_ret[:, l], 'ssd': state_ssd[:, l]}
        xs, _ = trunk_layer(xs, c, layer_params(l), ctx)

    return (xp, xs, new_gqa_k, new_gqa_v, new_swa_k, new_swa_v, new_state_ret, new_state_ssd)


_drawn_inputs = setup_inputs


def setup_inputs(seed=0):
    import zlib

    import numpy as np

    out = dict(_drawn_inputs(seed))
    spreads = {}
    factors = {'cache_gqa_k': 8.0,
     'cache_gqa_v': 8.0,
     'cache_swa_k': 8.0,
     'cache_swa_v': 8.0,
     'state_ret': 8.0,
     'ret_gn_g': 35.153,
     'gqa_q_norm': 8.0,
     'gqa_k_norm': 8.793,
     'ssd_d': 64.0,
     'ssd_norm_g': 23.82,
     'swa_sink': 31.141}
    for name, (base, spread) in spreads.items():
        noise = np.random.default_rng([zlib.crc32(name.encode()), seed]).standard_normal(out[name].shape)
        drawn = base * np.exp(spread * noise) if base else spread * noise
        out[name] = __import__('jax').numpy.asarray(drawn.astype(out[name].dtype))
    for name, factor in factors.items():
        out[name] = (out[name] * factor).astype(out[name].dtype)
    return out
```

```python
from contextlib import ExitStack

import numpy as np

import concourse.bass as bass
from concourse import mybir

F32 = mybir.dt.float32
F32R = mybir.dt.float32r
ACT = mybir.ActivationFunctionType
ALU = mybir.AluOpType
AX = mybir.AxisListType.X

DM, DEPTH, HD, P = 1024, 2, 64, 128
CTX, LAT = 128, 512
TOK = CTX + LAT
NT = TOK // P
LT = LAT // P
CT = LT
KD = DM // P
HALF = TOK // 2
GRID_W = 64
THETA = 10000.0
LN_DVE = 2
LN_ORDER = [3, 4, 0, 1, 2]
WARM = 10
MIX_ORDER = [2, 3, 4, 5, 6, 7, 0, 1]
DFF = -(-(8 * DM) // (3 * 256)) * 256
NFF = DFF // P
NMOD = 6 * DM // P
ALPHA = (2.0 * DEPTH) ** 0.25
SCALE = HD ** -0.5
NEG = -1.0e30
GRID = LAT + 3 * P

IN_SLABS = [("x", [(1792, 2048)], False), ("b", [(2048, 2304)], False), ("c", [(2304, 2560)], False),
            ("z", [(1536, 1792), (2560, 2568)], True), ("wq", [(2568, 2824)], True), ("wkv", [(2824, 3080)], True),
            ("gq", [(1024, 1280)], True), ("gkv", [(1280, 1536)], True), ("rq", [(0, 256)], False),
            ("rk", [(256, 512)], False), ("rv", [(512, 768)], True), ("rg", [(768, 1024)], True)]
NIN = len(IN_SLABS)
BEFORE_SSD = 6
FF_PARTS = [8, 8, 6]
ADA_FIRST = KD
ADA_IN = 3 * KD // 2
ADA_GATE = KD // 2
RAW_COLS = KD * 264

GROUPS_BEFORE = [0]
for _, _, _tok in IN_SLABS:
    GROUPS_BEFORE.append(GROUPS_BEFORE[-1] + (NT if _tok else 4))
K_OUT = NIN
K_FF = [K_OUT + KD]
K_DN = []
for _n in FF_PARTS:
    K_DN.append(K_FF[-1] + _n)
    K_FF.append(K_DN[-1] + KD)
K_ALL = K_FF[-1]

CONSTS = [("ident", P), ("ones", P), ("upper", P), ("lower", P), ("supper", P), ("slower", P), ("before", P),
          ("after", P), ("cos", LT * HD), ("sin", LT * HD), ("kpos", 8), ("dist", GRID), ("row", LAT)]
CONST_AT, _n = {}, 0
for _name, _w in CONSTS:
    CONST_AT[_name] = (_n, _n + _w)
    _n += _w
CONST_COLS = _n


def constants():
    out = np.zeros((P, CONST_COLS), np.float32)

    def put(name, a):
        lo, hi = CONST_AT[name]
        out[:, lo:hi] = a

    i, j = np.arange(P)[:, None], np.arange(P)[None, :]
    put("ident", i == j)
    put("ones", 1.0)
    put("upper", i <= j)
    put("lower", i >= j)
    put("supper", i < j)
    put("slower", i > j)
    put("before", np.where(j >= i, 0.0, NEG))
    put("after", np.where(j <= i, 0.0, NEG))
    n = np.arange(LAT)
    quarter = HD // 4
    freq = (THETA ** (-np.arange(quarter, dtype=np.float32) / quarter)).astype(np.float32)
    rows, cols = (n // GRID_W).astype(np.float32), (n % GRID_W).astype(np.float32)
    ang = [rows[:, None] * freq, cols[:, None] * freq]
    cos = np.concatenate([np.cos(ang[0])] * 2 + [np.cos(ang[1])] * 2, 1)
    sin = np.concatenate([-np.sin(ang[0]), np.sin(ang[0]), -np.sin(ang[1]), np.sin(ang[1])], 1)
    put("cos", cos.reshape(LT, P, HD).transpose(1, 0, 2).reshape(P, LT * HD))
    put("sin", sin.reshape(LT, P, HD).transpose(1, 0, 2).reshape(P, LT * HD))
    p = np.arange(P)[:, None]
    put("kpos", np.concatenate([np.repeat(P - 1 - p, 4, 1), np.repeat(p, 4, 1)], 1))
    put("dist", np.arange(GRID)[None, :] - 3 * P - p)
    put("row", np.arange(LAT)[None, :] + 1.0)
    return out


def build(nc, x_prompt, x_sample, cache_gqa_k, cache_gqa_v, cache_swa_k, cache_swa_v, state_ret, state_ssd,
          c, c_ctx, ada_w, ada_b, w_in, ret_decay, ret_gn_g, gqa_q_norm, gqa_k_norm, ssd_conv_w, ssd_conv_b,
          ssd_dt_bias, ssd_a_log, ssd_d, ssd_norm_g, swa_sink, w_out, ln1_g, ln1_b, w_ffn_in, w_ffn_out,
          ln2_g, ln2_b, consts, y_prompt, y_sample, new_gqa_k, new_gqa_v, new_swa_k, new_swa_v, new_ret, new_ssd):
    ctx = ExitStack()
    x_hold = nc.dram_tensor("x_hold", (P, NT * DM), F32, kind="Internal").ap()

    base = nc.sbuf_base + 31 & ~31
    room = nc.sbuf_usable_end
    names = set()

    def at(offset, name, cols, dt=F32, rows=P):
        assert name not in names and offset + cols * 4 <= room, (name, offset + cols * 4, room)
        names.add(name)
        return nc.alloc_sbuf_tensor_at(name, [rows, cols], dt, offset=offset)

    def fixed(name, cols, dt=F32, rows=P):
        nonlocal base
        t = at(base, name, cols, dt, rows)
        base += cols * 4 + 31 & ~31
        return t

    cst = fixed("cst", CONST_COLS)
    h_hi = fixed("h_hi", KD * TOK, F32R)[:].rearrange("p (k t) -> p k t", k=KD)
    h_lo = fixed("h_lo", KD * TOK, F32R)[:].rearrange("p (k t) -> p k t", k=KD)
    raw = [fixed(f"raw{i}", RAW_COLS)[:] for i in range(2)]
    w_hi = [fixed(f"w_hi{i}", RAW_COLS, F32R)[:] for i in range(2)]
    w_lo = [fixed(f"w_lo{i}", RAW_COLS, F32R)[:] for i in range(2)]
    prow = fixed("prow", P, rows=88)
    pcol = fixed("pcol", 88)
    cond = fixed("cond", 16)
    ln_fold = fixed("ln_fold", 2 * KD)
    mod_next = fixed("mod_next", 2 * KD * 2)[:].rearrange("p (m c) -> p m c", c=2)
    gates = fixed("gates", 4)[:].rearrange("p (b c) -> p b c", b=2)
    mod = fixed("mod", NMOD * 2)[:].rearrange("p (m c) -> p m c", c=2)
    qk_gain = fixed("qk_gain", 384)
    norm_g = fixed("norm_g", 256)
    gn_g = fixed("gn_g", 256)
    ck = [fixed(f"ck{i}", P) for i in range(2)]
    s0 = fixed("s0", 256)[:].rearrange("p (r j e) -> p r j e", r=2, j=2)
    decay = fixed("decay", 12)
    dec = fixed("dec", 5 * 12)[:].rearrange("p (i n) -> p i n", i=5)
    dec513 = fixed("dec513", 2)
    dt_bias = fixed("dt_bias", 8)
    a_log = fixed("a_log", 8)
    skip_d = fixed("skip_d", 4)
    sink = fixed("sink", 4)
    nsink = fixed("nsink", 4)
    arena = base

    def region(start):
        here = [arena + start]

        def put(name, cols, dt=F32, rows=P):
            t = at(here[0], name, cols, dt, rows)[:]
            here[0] += cols * 4 + 31 & ~31
            return t
        return put, here

    r0, at0 = region(0)
    w_qk = r0("w_qk", NT * 384).rearrange("p (t c) -> p t c", t=NT)
    w_v = r0("w_v", 6 * P).rearrange("p (t c) -> p t c", t=6)
    g_qk = r0("g_qk", NT * 384).rearrange("p (t c) -> p t c", t=NT)
    g_v = r0("g_v", 6 * P).rearrange("p (t c) -> p t c", t=6)
    mix_s = r0("mix_s", NT * 256).rearrange("p (t c) -> p t c", t=NT)
    after0 = at0[0] - arena

    PAD = TOK + 4
    CON = LAT + 2
    r1, at1 = region(after0)
    xbc_in = r1("xbc_in", 6 * PAD).rearrange("p (m t) -> p m t", m=6)
    after_xbc = at1[0] - arena
    z_act = r1("z_act", NT * 256).rearrange("p (t c) -> p t c", t=NT)
    dt_in = r1("dt_in", NT * 8)
    xbc = r1("xbc", 6 * PAD).rearrange("p (m t) -> p m t", m=6)
    at_xb = at1[0] - arena
    xb = r1("xb", NT * 512).rearrange("p (t c) -> p t c", t=NT)
    hst = r1("hst", 2 * LT * 256).rearrange("p (r s c) -> p r s c", r=2, s=LT)
    dam = r1("dam", 2 * 512).rearrange("p (b c) -> p b c", b=2)
    seg = r1("seg", 512)
    ada_in_slot = [at(arena + o, f"ada_in_slot{i}", KD * 256)[:] for i, o in enumerate((70144, 78336))]
    at_sm = at1[0] - arena
    sm = r1("sm", 512).rearrange("p (r c) -> p r c", r=2)
    pr = r1("pr", 2 * 512).rearrange("p (r c) -> p r c", r=2)
    yi = r1("yi", 512)
    small = r1("small", 20 * 40).rearrange("p (i c) -> p i c", i=20)
    r2, _ = region(after0)
    xdt = r2("xdt", 2 * NT * 256).rearrange("p (r t c) -> p r t c", r=2, t=NT)
    xw = r2("xw", NT * 256).rearrange("p (t c) -> p t c", t=NT)
    assert _[0] - arena <= after_xbc
    r2, _ = region(at_xb)
    ssq = r2("ssq", NT * 256).rearrange("p (t c) -> p t c", t=NT)
    hrow = at(arena + at_sm, "hrow", 512)[:]

    r3, at3 = region(after0)
    mix_w = r3("mix_w", NT * 256).rearrange("p (t c) -> p t c", t=NT)
    mix_g = r3("mix_g", NT * 256).rearrange("p (t c) -> p t c", t=NT)
    mix_r = r3("mix_r", NT * 256).rearrange("p (t c) -> p t c", t=NT)
    rqT = r3("rqT", 2 * TOK).rearrange("p (j t) -> p j t", j=2)
    rkT = r3("rkT", 2 * TOK).rearrange("p (j t) -> p j t", j=2)
    r_v = r3("r_v", NT * 256).rearrange("p (t c) -> p t c", t=NT)
    r_g = r3("r_g", NT * 256).rearrange("p (t c) -> p t c", t=NT)
    after3 = at3[0] - arena
    qkr = r3("qkr", NT * 384).rearrange("p (t c) -> p t c", t=NT)
    qkT = r3("qkT", 3 * 768).rearrange("p (j t) -> p j t", j=3)
    probs = r3("probs", 2 * TOK).rearrange("p (b c) -> p b c", b=2)
    pT = r3("pT", 2 * TOK).rearrange("p (b k q) -> p b k q", b=2, q=P)
    rowsum = r3("rowsum", 5 * 4 * NT).rearrange("p (i t h) -> p i t h", i=5, h=4)
    r4, at4 = region(after3)
    rqd = r4("rqd", 2 * 2 * LAT).rearrange("p (r j t) -> p r j t", r=2, j=2)
    toep = r4("toep", 2 * GRID).rearrange("p (b c) -> p b c", b=2)
    rctx = r4("rctx", 4 * P).rearrange("p (h q) -> p h q", h=4)
    rpT = r4("rpT", 2 * LT * LAT).rearrange("p (b k q) -> p b k q", b=2, k=LT)
    r_o = r4("r_o", NT * 256).rearrange("p (t c) -> p t c", t=NT)
    r4b, _ = region(GRID * 4 + 31 & ~31)
    rsq = r4b("rsq", NT * HD).rearrange("p (t d) -> p t d", t=NT)
    rstat = r4b("rstat", 4 * 20).rearrange("p (i c) -> p i c", i=4)
    r4c, _ = region(0)
    toep_b = r4c("toep_b", GRID)
    r4d, _ = region(NT * 384 * 4 + 6 * P * 4)
    kd = r4d("kd", 512).rearrange("p (r c) -> p r c", r=2)
    rst_out = r4d("rst_out", 512)
    kexp = r4d("kexp", 8)
    ret_oT = r4d("ret_oT", 2 * LAT).rearrange("p (b t) -> p b t", b=2)
    assert _[0] - arena <= 2 * (NT * 384 + 6 * P) * 4
    r7, _ = region(after3 + 27136 + 512)
    rope_a = r7("rope_a", 384)
    rope_b = r7("rope_b", 384)
    g_st = r7("g_st", 3 * 30).rearrange("p (i c) -> p i c", i=3)
    r8, _ = region(after0)
    gsq = r8("gsq", NT * 384).rearrange("p (t c) -> p t c", t=NT)
    sst_out = at(arena + at0[0] - arena - NT * 256 * 4, "sst_out", 512)[:]

    x_at = (room - arena - NT * DM * 4) & ~31
    ln_at = x_at - 2 * DM * 4
    x = at(arena + x_at, "x", NT * DM)[:].rearrange("p (t d) -> p t d", t=NT)
    ln_gb = at(arena + ln_at, "ln_gb", 2 * DM)[:].rearrange("p (i d) -> p i d", i=2)
    r5, at5 = region(0)
    NP = max(FF_PARTS)
    a_hi = r5("a_hi", NP * TOK, F32R).rearrange("p (k t) -> p k t", k=NP)
    a_lo = r5("a_lo", NP * TOK, F32R).rearrange("p (k t) -> p k t", k=NP)
    sg = r5("sg", 2 * TOK).rearrange("p (b t) -> p b t", b=2)
    act_ = r5("act_", 2 * TOK).rearrange("p (b t) -> p b t", b=2)
    assert at5[0] - arena <= ln_at
    ada_ff_slot = at(at5[0] + 2 * TOK * 4, "ada_ff_slot", KD * 256)[:]
    back = r5("back", 2 * TOK).rearrange("p (b t) -> p b t", b=2)
    r6, at6 = region(ln_at - (2 * TOK + NT * 24 + NT * 2 + 3 * NT) * 4 - 128 & ~31)
    assert at5[0] + KD * 256 * 4 <= at6[0] and arena + after3 <= at6[0], (at5[0] - arena, at6[0] - arena)
    first_slab = [at(arena + i * KD * 256 * 4, f"first_slab{i}", KD * 256)[:] for i in range(ADA_FIRST)]
    hmid = r6("hmid", 2 * TOK).rearrange("p (b t) -> p b t", b=2)
    ln_st = r6("ln_st", NT * 24).rearrange("p (t c) -> p t c", t=NT)
    ln_mv = r6("ln_mv", NT * 2).rearrange("p (t c) -> p t c", t=NT)
    ln_r = r6("ln_r", 3 * NT).rearrange("p (i t) -> p i t", i=3)
    assert at6[0] - arena <= ln_at, (at6[0] - arena, ln_at)

    def k_(name):
        lo, hi = CONST_AT[name]
        return cst[:, lo:hi]

    ident, ones, upper, lower = k_("ident"), k_("ones"), k_("upper"), k_("lower")

    ps = ctx.enter_context(nc.psum_tensor("ps", [P, 8 * 512], F32))[:]
    bank = [ps[:, 512 * b:512 * (b + 1)] for b in range(8)]

    sems = {}

    def sem(name):
        sems[name] = ctx.enter_context(nc.semaphore(name))
        return sems[name]

    start_in = sem("start_in")
    params_in = sem("params_in")
    x_spilled = sem("x_spilled")
    x_back = sem("x_back")
    ln_in = [sem("ln1_in"), sem("ln2_in")]
    raw_in = [sem("raw_in0"), sem("raw_in1")]
    ada_in = [sem("ada_in0"), sem("ada_in1"), sem("ada_in_ff")]
    ada_used = sem("ada_used")
    prow_in = sem("prow_in")
    hi_ready = sem("hi_ready")
    lo_ready = sem("lo_ready")
    sst_sent = sem("sst_sent")
    params_turned = sem("params_turned")
    params_ready = sem("params_ready")
    cond_ready = sem("cond_ready")
    mod_ready = sem("mod_ready")
    fm_turned = sem("fm_turned")
    fm_mid = sem("fm_mid")
    h_ready = sem("h_ready")
    in_done = sem("in_done")
    in_out = sem("in_out")
    pool_pads = sem("pool_pads")
    conv_mid = sem("conv_mid")
    conv_acc = sem("conv_acc")
    conv_out = sem("conv_out")
    sp_d = sem("softplus_dve")
    sp_a = sem("softplus_act")
    dt_ready = sem("dt_ready")
    cum_done = sem("cum_done")
    decays_act = sem("decays_act")
    decays_dve = sem("decays_dve")
    ssd_turned = sem("ssd_turned")
    ssd_rows = sem("ssd_rows")
    xdt_ready = sem("xdt_ready")
    xw_ready = sem("xw_ready")
    upd_done = sem("upd_done")
    st_ready = sem("st_ready")
    sc_done = sem("sc_done")
    sm_ready = sem("sm_ready")
    dam_ready = sem("dam_ready")
    seg_done = sem("seg_done")
    seg_exp = sem("seg_exp")
    pr_ready = sem("pr_ready")
    y_done = sem("y_done")
    y_out = sem("y_out")
    skip_ready = sem("skip_ready")
    ssd_gated = sem("ssd_gated")
    rms_act = sem("rms_act")
    mix_ready = sem("mix_ready")
    roped = sem("roped")
    g_normed = sem("g_normed")
    g_rms = sem("g_rms")
    qk_turned = sem("qk_turned")
    qk_ready = sem("qk_ready")
    s_done = sem("s_done")
    nmax_ready = sem("nmax_ready")
    probs_ready = sem("probs_ready")
    pT_done = sem("pT_done")
    pTa_ready = sem("pTa_ready")
    pTb_ready = sem("pTb_ready")
    o_done = sem("o_done")
    o_out = sem("o_out")
    sink_exp = sem("sink_exp")
    sink_sum = sem("sink_sum")
    ret_d = sem("ret_dve")
    ret_a = sem("ret_act")
    ret_qd = sem("ret_qd")
    ret_s = sem("ret_scores")
    ret_p = sem("ret_probs")
    ret_o = sem("ret_o")
    ret_k = sem("ret_k")
    ret_kd = sem("ret_kd")
    ret_st = sem("ret_state")
    ret_sto = sem("ret_state_out")
    ret_v = sem("ret_values")
    ret_ot = sem("ret_values_out")
    ret_norm = sem("ret_norm")
    ret_gate = sem("ret_gate")
    back_done = sem("back_done")
    back_ready = sem("back_ready")
    back_turned = sem("back_turned")
    res_added = sem("res_added")
    gates_ready = sem("gates_ready")
    ln_d = sem("ln_dve")
    ln_a = sem("ln_act")
    ln_out = sem("ln_out")
    ln_folded = sem("ln_folded")
    ln_hat = sem("ln_hat")
    ln_centred = sem("ln_centred")
    gate_done = sem("gate_done")
    up_done = sem("up_done")
    silu_ready = sem("silu_ready")
    act_ready = sem("act_ready")
    ahi_ready = sem("ahi_ready")
    alo_ready = sem("alo_ready")
    out_sent = sem("out_sent")
    dve_step = sem("dve_step")
    pool_step = sem("pool_step")
    y_sent = sem("y_sent")
    numbers = sorted(s.num for s in sems.values())
    assert numbers[-1] - numbers[0] == len(numbers) - 1

    crow = prow[0:16, :]
    ada_v = ada_w.rearrange("l (k p) c -> p (l k) c", p=P)
    with nc.Block() as block:
        @block.sync
        def _(sp):
            sp.dma_start(cst[:, 0:P], consts[:, 0:P]).then_inc(prow_in, 16)
            sp.dma_start(prow[0:8, :], c[0].rearrange("(k p) -> k p", p=P)).then_inc(prow_in, 16)
            sp.dma_start(prow[8:16, :], c_ctx.rearrange("(k p) -> k p", p=P)).then_inc(prow_in, 16)
            for i in range(ADA_FIRST):
                sp.dma_start(first_slab[i].rearrange("p (k c) -> p k c", k=KD),
                             ada_v[:, 0:KD, i * 256:(i + 1) * 256]).then_inc(ada_in[0], 16)
            sp.dma_start(x[:, 0:LT, :], x_sample[0].rearrange("(t p) d -> p t d", p=P)).then_inc(start_in, 16)
            sp.dma_start(x[:, CT, :], x_prompt[0]).then_inc(start_in, 16)
            sp.dma_start(cst[:, P:CONST_COLS], consts[:, P:CONST_COLS]).then_inc(start_in, 16)
            sp.wait_ge(start_in, 48)

        @block.tensor
        def _(pe):
            pe.wait_ge(prow_in, 48)
            pe.transpose(bank[5][:, 0:16], crow, ident[0:16, 0:16]).then_inc(params_turned, 1)
            pe.wait_ge(cond_ready, 1)
            pe.wait_ge(ada_in[0], 16 * ADA_FIRST)
            for i in range(ADA_FIRST):
                w = first_slab[i].rearrange("p (k c) -> p k c", k=KD)
                for mm in range(2):
                    m = 2 * i + mm
                    for k in range(KD):
                        last = pe.matmul(bank[6][:, 2 * m:2 * m + 2], w[:, k, mm * P:(mm + 1) * P],
                                         cond[:, k:16:KD], start=k == 0, stop=k == KD - 1)
            last.then_inc(ada_used, 1)

        @block.scalar
        def _(ac):
            ac.wait_ge(params_turned, 1)
            ac.activation(cond[:], bank[5][:, 0:16], ACT.Silu).then_inc(cond_ready, 1)

        @block.vector
        def _(ve):
            ve.wait_ge(ada_used, 1)
            ve.tensor_copy(mod_next, bank[6][:, 0:4 * KD].rearrange("p (m c) -> p m c", c=2)).then_inc(mod_ready, 1)
            ve.wait_ge(mod_ready, 1)

    def slab(t, nk, cols):
        return t[:, 0:nk * cols].rearrange("p (k c) -> p k c", k=nk)

    START = 1
    NEXT = DEPTH - 1
    assert DEPTH == 2
    ADA_BESIDE = [ADA_IN, ADA_IN + ADA_GATE, ADA_IN + ADA_GATE + KD // 2 + 1]

    def ada_slot(a):
        return ada_in_slot[a % 2] if 0 < a < ADA_IN else ada_ff_slot

    PARAM_DMAS = 21
    SENDS = 5
    layer_loop = nc.Fori(0, DEPTH)
    l = layer_loop.__enter__()
    nc.all_engine_barrier(sems_to_clear=range(numbers[0], numbers[-1] + 1))
    with nc.Block() as block:

        @block.sync
        def _(sp):
            n_param = [0]

            def param(out, in_):
                sp.dma_start(out, in_).then_inc(params_in, 16)
                n_param[0] += 1

            def lrow(a):
                return a[bass.ds(l, 1), :]

            def load(k, out, in_, first=True):
                if k >= 2 and first:
                    sp.wait_ge(lo_ready, k - 1)
                sp.dma_start(out, in_).then_inc(raw_in[k % 2], 16)

            in_v = w_in.rearrange("l (k p) c -> p (l k) c", p=P)

            def load_in(k):
                parts = IN_SLABS[k][1]
                at_col, width = 0, sum(b - a for a, b in parts)
                for n, (a, b) in enumerate(parts):
                    load(k, slab(raw[k % 2], KD, width)[:, :, at_col:at_col + b - a],
                         in_v[:, bass.ds(l * KD, KD), a:b], first=n == 0)
                    at_col += b - a

            def load_ada(a):
                if a >= 2:
                    sp.wait_ge(ada_used, a - 1)
                m = 2 * KD + 2 * a
                sp.dma_start(slab(ada_slot(a), KD, 256),
                             ada_v[:, bass.ds(l * KD, KD), m * P:(m + 2) * P]).then_inc(ada_in[a % 2], 16)

            def turned_param(out, in_):
                sp.dma_start(out, in_).then_inc(prow_in, 16)

            turned_param(prow[0:48, :], ada_b.rearrange("l (k p) -> (l k) p", p=P)[bass.ds(l * NMOD, NMOD), :])
            turned_param(prow[48:66, :], ssd_conv_w.rearrange("l k (m p) -> (l k m) p", p=P)[bass.ds(l * 18, 18), :])
            turned_param(prow[66:72, :], ssd_conv_b.rearrange("l (m p) -> (l m) p", p=P)[bass.ds(l * 6, 6), :])
            turned_param(prow[72:80, :], ln1_g.rearrange("l (k p) -> (l k) p", p=P)[bass.ds(l * KD, KD), :])
            turned_param(prow[80:88, :], ln1_b.rearrange("l (k p) -> (l k) p", p=P)[bass.ds(l * KD, KD), :])
            load_in(0)
            load_in(1)
            load_ada(0)
            sp.dma_start(x_hold, x.rearrange("p t d -> p (t d)")).then_inc(x_spilled, 16)
            for h in range(4):
                param(qk_gain[:, h * HD:(h + 1) * HD], lrow(gqa_q_norm).to_broadcast([P, HD]))
            for h in range(4, 6):
                param(qk_gain[:, h * HD:(h + 1) * HD], lrow(gqa_k_norm).to_broadcast([P, HD]))
            param(norm_g[:], lrow(ssd_norm_g).to_broadcast([P, 256]))
            param(gn_g[:], lrow(ret_gn_g).to_broadcast([P, 256]))
            param(decay[:, 0:8], lrow(ret_decay.rearrange("l r h -> l (r h)")).to_broadcast([P, 8]))
            for g in range(2):
                v = ret_decay.rearrange("l r (j g) -> l g (r j)", g=2)[bass.ds(l, 1), g, :]
                with nc.allow_non_contiguous_dma(reason="four decays"):
                    param(decay[g * HD:(g + 1) * HD, 8:12], v.to_broadcast([HD, 4]))
            param(dt_bias[:], lrow(ssd_dt_bias.rearrange("l r h -> l (r h)")).to_broadcast([P, 8]))
            param(a_log[:], lrow(ssd_a_log.rearrange("l r h -> l (r h)")).to_broadcast([P, 8]))
            param(skip_d[:], lrow(ssd_d).to_broadcast([P, 4]))
            param(sink[:], lrow(swa_sink).to_broadcast([P, 4]))
            for i, (kc, vc, v) in enumerate(((cache_swa_k, cache_swa_v, w_v), (cache_gqa_k, cache_gqa_v, g_v))):
                param(ck[i][:], kc[0, bass.ds(l, 1)].rearrange("l s h d -> s (l h d)"))
                param(v[:, 5, :], vc[0, bass.ds(l, 1)].rearrange("l s h d -> s (l h d)"))
            sr = state_ret[0].rearrange("l r (j g) d e -> g l d (r j) e", g=2)
            for g in range(2):
                param(s0[g * HD:(g + 1) * HD], sr[g, bass.ds(l, 1)].rearrange("l d n e -> d (l n) e"))
            assert n_param[0] == PARAM_DMAS, n_param
            for k in range(NIN):
                if k >= 2 and k != BEFORE_SSD + 1:
                    load_in(k)
                if k == 1:
                    sp.wait_ge(x_spilled, 16)
                    sp.wait_ge(h_ready, KD)
                if k == 2:
                    sp.dma_start(hrow.rearrange("p (r g n) -> p r g n", r=2, g=2),
                                 state_ssd[0, bass.ds(l, 1)].rearrange("l r (g h) p n -> (l h p) r g n", g=2)
                                 ).then_inc(ssd_rows, 16)
                if k == BEFORE_SSD:
                    load_in(k + 1)
                    sp.wait_ge(skip_ready, 1)
                if k >= 1:
                    load_ada(k)
            out_v = w_out.rearrange("l (k p) c -> p (l k) c", p=P)
            for m in range(KD):
                k = K_OUT + m
                load(k, slab(raw[k % 2], KD, P), out_v[:, bass.ds(l * KD, KD), m * P:(m + 1) * P])
                if m == 1:
                    sp.wait_ge(h_ready, 2 * KD)
                    sp.dma_start(x.rearrange("p t d -> p (t d)"), x_hold).then_inc(x_back, 16)
                    sp.dma_start(ln_gb[:, 0, :], lrow(ln1_g).to_broadcast([P, DM])).then_inc(ln_in[0], 16)
                    sp.dma_start(ln_gb[:, 1, :], lrow(ln1_b).to_broadcast([P, DM])).then_inc(ln_in[0], 16)
            up_v = w_ffn_in.rearrange("l (k p) (u c) -> p (l k) u c", p=P, u=2)
            dn_v = w_ffn_out.rearrange("l (k p) c -> p (l k) c", p=P)
            first_ff = 0
            for part, nf in enumerate(FF_PARTS):
                with sp.Fori(0, (nf) // 2) as pair:
                    i = pair * 2
                    for b in range(2):
                        sp.wait_ge(lo_ready, i + (K_FF[part] + b - 1))
                        dst = raw[b][:, 0:KD * 2 * P].rearrange("p (k u c) -> p k u c", k=KD, u=2)
                        for u in range(2):
                            sp.dma_start(dst[:, :, u, :],
                                         up_v[:, bass.ds(l * KD, KD), u, bass.ds(i * P + (first_ff + b) * P, P)]
                                         ).then_inc(raw_in[b], 16)
                    sp.wait_ge(ada_used, pair + ADA_BESIDE[part])
                    if part == 0:
                        rows, col = bass.ds(l * KD, KD), bass.ds(i * P + 5 * KD * P, 256)
                    else:
                        rows, col = slice(NEXT * KD, (NEXT + 1) * KD), bass.ds(i * P + (0, 0, KD + 2)[part] * P, 256)
                    sp.dma_start(slab(ada_ff_slot, KD, 256), ada_v[:, rows, col]).then_inc(ada_in[2], 16)
                if part == 0:
                    sp.wait_ge(ln_out, NT)
                    sp.dma_start(ln_gb[:, 0, :], lrow(ln2_g).to_broadcast([P, DM])).then_inc(ln_in[1], 16)
                    sp.dma_start(ln_gb[:, 1, :], lrow(ln2_b).to_broadcast([P, DM])).then_inc(ln_in[1], 16)
                with sp.Fori(0, (KD) // 2) as pair:
                    m = pair * 2
                    for b in range(2):
                        sp.wait_ge(lo_ready, m + (K_DN[part] + b - 1))
                        sp.dma_start(slab(raw[b], nf, P),
                                     dn_v[:, bass.ds(l * NFF + first_ff, nf), bass.ds(m * P + b * P, P)]
                                     ).then_inc(raw_in[b], 16)
                if part == 1:
                    sp.wait_ge(ada_used, ADA_BESIDE[2] - 1)
                    sp.dma_start(slab(ada_ff_slot, KD, 256),
                                 ada_v[:, NEXT * KD:(NEXT + 1) * KD, KD * P:KD * P + 256]).then_inc(ada_in[2], 16)
                first_ff += nf

        def raw_count(k):
            total = 0
            for q in range(k % 2, k + 1, 2):
                if q < NIN:
                    total += 16 * len(IN_SLABS[q][1])
                elif any(K_FF[i] <= q < K_DN[i] for i in range(len(FF_PARTS))):
                    total += 32
                else:
                    total += 16
            return total

        def slab_size(k):
            if k < NIN:
                return KD * sum(b - a for a, b in IN_SLABS[k][1])
            for i, nf in enumerate(FF_PARTS):
                if K_FF[i] <= k < K_DN[i]:
                    return KD * 2 * P
                if K_DN[i] <= k < K_FF[i + 1]:
                    return nf * P
            return KD * P

        def slab_read(eng, k):
            if k < NIN:
                return eng.wait_ge(in_done, GROUPS_BEFORE[k + 1])
            if k < K_FF[0]:
                return eng.wait_ge(back_done, 2 * (k - K_OUT + 1) + START)
            ff = 0
            for i, nf in enumerate(FF_PARTS):
                if k < K_DN[i]:
                    return eng.wait_ge(up_done, 2 * (ff + k - K_FF[i] + 1) + START)
                if k < K_FF[i + 1]:
                    return eng.wait_ge(back_done, 2 * ((i + 1) * KD + k - K_DN[i] + 1) + START)
                ff += nf

        def split_hi(eng, k, i=None, read=None, before=0):
            n, b = slab_size(k), k % 2
            if i is None:
                eng.wait_ge(raw_in[b], raw_count(k))
                if k >= 2:
                    slab_read(eng, k - 2)
            else:
                per_slab = raw_count(k + 2) - raw_count(k)
                eng.wait_ge(raw_in[b], i * (per_slab // 2) + raw_count(k))
                eng.wait_ge(read, i * 2 + before)
            eng.activation(w_hi[b][:, 0:n], raw[b][:, 0:n], ACT.Copy).then_inc(hi_ready, 1)

        def split_lo(eng, k, i=None):
            n, b = slab_size(k), k % 2
            eng.wait_ge(hi_ready, k + 1 if i is None else i + (k + 1))
            eng.tensor_tensor(w_lo[b][:, 0:n], raw[b][:, 0:n], w_hi[b][:, 0:n].bitcast(F32),
                              ALU.subtract).then_inc(lo_ready, 1)

        items = [(t, h) for t in range(NT) for h in range(4)]

        def keys_of(kind, t):
            if t == CT:
                return [(LAT, P, [CT])]
            if kind == "g":
                return [(0, LAT, [0, 1, 2, 3]), (TOK, P, [5])]
            a, b = max(t - 1, 0), min(t + 1, LT - 1)
            return [(a * P, (b + 1 - a) * P, list(range(a, b + 1))), (TOK, P, [5])]

        def key_count(kind, t):
            return sum(len(v) for _, _, v in keys_of(kind, t))

        has_b = [[key_count(kind, t) > 4 for t, h in items] for kind in "wg"]
        nb_before = [[sum(hb[:i]) for i in range(len(items) + 1)] for hb in has_b]
        NI = len(items)

        @block.tensor
        def _(pe):
            freed = {}

            def take(b, by, value):
                if b in freed:
                    pe.wait_ge(*freed[b])
                freed[b] = (by, value)

            pe.sem_inc(back_done, START)
            pe.sem_inc(up_done, START)
            def turn_parameters():
                pe.wait_ge(prow_in, 80)
                take(3, params_ready, 1)
                pe.transpose(bank[3][:, 0:88], prow[:], ident[0:88, 0:88]).then_inc(params_turned, 1)

            def modulate(a, quarter, pair=None):
                if quarter > 3:
                    return
                in_ff = a >= ADA_IN
                if quarter == 0:
                    landed = 16 * (a - ADA_IN + 1) if in_ff else 16 * (a // 2 + 1)
                    pe.wait_ge(ada_in[2 if in_ff else a % 2], landed if pair is None else pair * 16 + landed)
                    read = a + 1 + (a >= ADA_IN + ADA_GATE)
                    if pair is None and a <= ADA_IN:
                        take(6, mod_ready, read + 1)
                    pe.wait_ge(mod_ready, read if pair is None else pair + read)
                w = slab(ada_slot(a), KD, 256)
                mm = quarter // 2
                for k in range(KD // 2 * (quarter % 2), KD // 2 * (quarter % 2 + 1)):
                    last = pe.matmul(bank[6][:, 2 * mm:2 * mm + 2], w[:, k, mm * P:(mm + 1) * P],
                                     cond[:, k:16:KD], start=k == 0, stop=k == KD - 1)
                if quarter == 3:
                    last.then_inc(ada_used, 1)

            def to_features(n, source):
                for k in range(KD):
                    i = n * KD + k
                    if i == 2:
                        turn_parameters()
                    take(4 + k % 2, fm_mid, i + 1)
                    take(6 + k % 2, fm_mid, i + 1)
                    for t in range(LT):
                        pe.transpose(bank[4 + k % 2][:, t * P:(t + 1) * P], source(t, k), ident)
                    pe.transpose(bank[6 + k % 2][:, 0:P], source(CT, k), ident).then_inc(fm_turned, 1)

            def x_tile(t, k):
                return x[:, t, k * P:(k + 1) * P]

            to_features(0, x_tile)

            def keep_warm(n):
                if 0 in freed:
                    pe.wait_ge(*freed[0])
                for _ in range(n):
                    pe.matmul(bank[0], ident, cst[:, 0:512], start=True, stop=True)

            def three(out, a_h, a_l, b_h, b_l, first, last):
                pe.matmul(out, a_h, b_h, start=first, stop=False)
                pe.matmul(out, a_h, b_l, start=False, stop=False)
                return pe.matmul(out, a_l, b_h, start=False, stop=last)

            def project(k):
                _, parts, tok = IN_SLABS[k]
                width = sum(b - a for a, b in parts)
                wh, wl = slab(w_hi[k % 2], KD, width), slab(w_lo[k % 2], KD, width)
                pe.wait_ge(lo_ready, k + 1)
                g = GROUPS_BEFORE[k]
                if tok:
                    for t in range(NT):
                        take(g % 4, in_out, g + 1)
                        cols = slice(t * P, (t + 1) * P)
                        for q in range(KD):
                            last = three(bank[g % 4][:, 0:width], h_hi[:, q, cols], h_lo[:, q, cols],
                                         wh[:, q, :], wl[:, q, :], q == 0, q == KD - 1)
                        last.then_inc(in_done, 1)
                        g += 1
                        if t:
                            modulate(k, t - 1)
                else:
                    for m in range(2):
                        for n in range(2):
                            take(g % 4, in_out, g + 1)
                            for q in range(KD):
                                cols, mc = slice(n * HALF, (n + 1) * HALF), slice(m * P, (m + 1) * P)
                                if k == m == n == 0:
                                    pe.wait_ge(h_ready, q + 1)
                                last = three(bank[g % 4][:, 0:HALF], wh[:, q, mc], wl[:, q, mc],
                                             h_hi[:, q, cols], h_lo[:, q, cols], q == 0, q == KD - 1)
                            last.then_inc(in_done, 1)
                            g += 1
                            modulate(k, 2 * m + n)

            def project_all(ks):
                for k in ks:
                    project(k)

            project_all(range(BEFORE_SSD))

            pe.wait_ge(conv_out, 4)
            pe.wait_ge(ssd_rows, 16)
            for m in range(4):
                take(4 + m, st_ready, m + 1)
                for t in range(LT):
                    last = pe.transpose(bank[4 + m][:, t * P:(t + 1) * P], xbc[:, m, t * P:(t + 1) * P], ident)
                last.then_inc(ssd_turned, 1)
            take(4, st_ready, 5)
            for m in range(4):
                last = pe.transpose(bank[4][:, m * P:(m + 1) * P], xbc[:, m, CON:CON + P], ident)
            last.then_inc(ssd_turned, 1)
            take(5, st_ready, 6)
            for i in range(4):
                last = pe.transpose(bank[5][:, i * P:(i + 1) * P], hrow[:, i * P:(i + 1) * P], ident)
            last.then_inc(ssd_turned, 1)
            pe.wait_ge(dt_ready, 1)
            take(6, decays_dve, 1)
            da = small[:, 0, :]
            pe.matmul(bank[6][:, 0:40], upper, da, start=True, stop=True)
            pe.matmul(bank[6][:, 40:80], lower, da, start=True, stop=True)
            pe.matmul(bank[6][:, 80:120], ones, da, start=True, stop=True).then_inc(cum_done, 1)
            keep_warm(WARM)
            n_upd = 0
            for r in range(2):
                pe.wait_ge(xw_ready, r + 1)
                pe.wait_ge(st_ready, 5)
                for t in ([0, 1, 2] if r == 0 else [3, 2, 1]):
                    n_upd += 1
                    take(4 + n_upd % 2, st_ready, 6 + n_upd)
                    for g in range(2):
                        last = pe.matmul(bank[4 + n_upd % 2][:, g * P:(g + 1) * P],
                                         xb[:, t, 256 + g * P:256 + (g + 1) * P], xw[:, t, g * P:(g + 1) * P],
                                         start=True, stop=True)
                    last.then_inc(upd_done, 1)
                n_upd += 1
                take(6 + r, st_ready, 6 + n_upd)
                for g in range(2):
                    last = pe.matmul(bank[6 + r][:, g * P:(g + 1) * P], xw[:, CT, g * P:(g + 1) * P],
                                     xb[:, CT, 256 + g * P:256 + (g + 1) * P], start=True, stop=True)
                last.then_inc(upd_done, 1)
            n_seg = 0
            for t in range(NT):
                cols = slice(CON, CON + P) if t == CT else slice(t * P, (t + 1) * P)
                take(0, sm_ready, 2 * (t + 1))
                if t == 0:
                    pe.wait_ge(conv_out, 6)
                for g in range(2):
                    last = pe.matmul(bank[0][:, g * P:(g + 1) * P], xbc[:, 2 + g, cols], xbc[:, 4 + g, cols],
                                     start=True, stop=True)
                last.then_inc(sc_done, 1)
                for r in range(2):
                    n_seg += 1
                    pe.wait_ge(dam_ready, n_seg)
                    take(1 + r, seg_exp, n_seg)
                    for h in range(4):
                        last = pe.matmul(bank[1 + r][:, h * P:(h + 1) * P], dam[:, r, h * P:(h + 1) * P],
                                         upper if r == 0 else lower, start=True, stop=True)
                    last.then_inc(seg_done, 1)
                if t < CT:
                    if t == 0:
                        pe.wait_ge(st_ready, 6 + 8)
                    take(3, y_out, t + 1)
                    for r in range(2):
                        for g in range(2):
                            pe.matmul(bank[3][:, r * 256 + g * P:r * 256 + (g + 1) * P], xbc[:, 4 + g, cols],
                                      hst[:, r, t, g * P:(g + 1) * P], start=True, stop=True)
                take(4 + t % 2, y_out, t + 1)
                pe.wait_ge(pr_ready, 2 * (t + 1))
                for h in range(4):
                    for r in range(2):
                        last = pe.matmul(bank[4 + t % 2][:, h * HD:(h + 1) * HD], pr[:, r, h * P:(h + 1) * P],
                                         xdt[:, r, t, h * HD:(h + 1) * HD], start=r == 0, stop=r == 1)
                last.then_inc(y_done, 1)

            project_all(range(BEFORE_SSD, NIN))

            for kind in range(2):
                name = "wg"[kind]
                pe.wait_ge(roped, NT * (kind + 1))
                for j in range(3):
                    take(4 + j, qk_ready, 4 * kind + j + 1)
                    for t in range(LT):
                        last = pe.transpose(bank[4 + j][:, t * P:(t + 1) * P], qkr[:, t, j * P:(j + 1) * P], ident)
                    last.then_inc(qk_turned, 1)
                take(7, qk_ready, 4 * kind + 4)
                for j in range(3):
                    pe.transpose(bank[7][:, j * P:(j + 1) * P], qkr[:, CT, j * P:(j + 1) * P], ident)
                pe.transpose(bank[7][:, 3 * P:4 * P], ck[kind][:], ident).then_inc(qk_turned, 1)
                keep_warm(WARM if kind else WARM // 2)
                pe.wait_ge(qk_ready, 4 * kind + 4)

                def scores(i):
                    t, h = items[i]
                    g, j = h // 2, h % 2
                    rows = slice(g * HD, (g + 1) * HD)
                    b0 = 2 * (i % 2)
                    q = qkT[rows, j, t * P:(t + 1) * P]
                    n = kind * NI + i
                    take(b0, probs_ready, n + 1)
                    wide = key_count(name, t) > 4
                    if wide:
                        take(b0 + 1, probs_ready, n + 1)
                    runs = keys_of(name, t)
                    a, w, tiles = runs[0]
                    masked = [(tiles.index(o), m) for o, m in ((t - 1, "before"), (t + 1, "after"))
                              if name == "w" and t != CT and o in tiles]
                    last = pe.matmul(bank[b0][:, 0:w], q, qkT[rows, 2, a:a + w], start=True, stop=True)
                    for z, (o, m) in enumerate(masked):
                        last = pe.matmul(bank[b0][:, o * P:(o + 1) * P], ident, k_(m), start=False,
                                         stop=True, skip_group_check=True)
                    if len(runs) > 1:
                        out = bank[b0 + 1][:, 0:P] if wide else bank[b0][:, w:w + P]
                        last = pe.matmul(out, q, qkT[rows, 2, TOK:TOK + P], start=True, stop=True)
                    last.then_inc(s_done, 1)

                def turn(i):
                    t, h = items[i]
                    n, nk = kind * NI + i, key_count(name, t)
                    pe.wait_ge(probs_ready, n + 1)
                    take(4, pTa_ready, n + 1)
                    for z in range(nk):
                        if z == 4:
                            take(5, pTb_ready, nb_before[kind][i] + 1)
                        out = bank[4][:, z * P:(z + 1) * P] if z < 4 else bank[5][:, 0:P]
                        last = pe.transpose(out, probs[:, i % 2, z * P:(z + 1) * P], ident)
                    last.then_inc(pT_done, 1)

                def values(i):
                    t, h = items[i]
                    n, g = kind * NI + i, h // 2
                    pe.wait_ge(pTa_ready, n + 1)
                    if has_b[kind][i]:
                        pe.wait_ge(pTb_ready, nb_before[kind][i] + 1)
                    if h == 0:
                        take(6 + t % 2, o_out, kind * NT + t + 1)
                    tiles = [v for run in keys_of(name, t) for v in run[2]]
                    vv = (w_v, g_v)[kind]
                    for z, v in enumerate(tiles):
                        last = pe.matmul(bank[6 + t % 2][:, h * HD:(h + 1) * HD], pT[:, i % 2, z, :],
                                         vv[:, v, g * HD:(g + 1) * HD], start=z == 0, stop=z == len(tiles) - 1)
                    last.then_inc(o_done, 1)

                scores(0)
                scores(1)
                for i in range(NI + 1):
                    if i < NI:
                        turn(i)
                    if i + 2 < NI:
                        scores(i + 2)
                    if i > 0:
                        values(i - 1)

            mixes = [mix_r, mix_g, mix_s, mix_w]

            def mix_turned(*ks):
                for k in ks:
                    i = KD + MIX_ORDER.index(k)
                    take(3, h_ready, i + 1)
                    take(4, h_ready, i + 1)
                    for t in range(NT):
                        last = pe.transpose(ps[:, 3 * 512 + t * P:3 * 512 + (t + 1) * P],
                                            mixes[k // 2][:, t, (k % 2) * P:(k % 2 + 1) * P], ident)
                    last.then_inc(fm_turned, 1)

            take(4, ret_kd, 2)
            for j in range(2):
                last = pe.transpose(bank[4][:, j * P:(j + 1) * P], rkT[:, j, LAT:TOK], ident)
            last.then_inc(ret_k, 1)
            n_rs = 0
            keep_warm(WARM)
            pe.wait_ge(ret_qd, 4)
            for h in range(4):
                j, rows = h // 2, slice((h % 2) * HD, (h % 2 + 1) * HD)
                for kt in range(NT):
                    n_rs += 1
                    b = 5 + n_rs % 2
                    take(b, ret_p, n_rs)
                    if kt < CT:
                        last = pe.matmul(bank[b][:, 0:LAT], rkT[rows, j, kt * P:(kt + 1) * P], rqT[rows, j, 0:LAT],
                                         start=True, stop=True)
                    else:
                        last = pe.matmul(bank[b][:, 0:P], rkT[rows, j, LAT:TOK], rqT[rows, j, LAT:TOK],
                                         start=True, stop=True)
                    last.then_inc(ret_s, 1)
                    if kt == LT - 1:
                        take(7, ret_ot, h + 1)
                        out = bank[7][0:HD, :]
                        for r in range(2):
                            pe.matmul(out, s0[rows, r, j, :], rqd[rows, r, j, :], start=r == 0, stop=False)
                        for q in range(LT):
                            pe.wait_ge(ret_p, h * NT + q + 1)
                            last = pe.matmul(out, r_v[:, q, h * HD:(h + 1) * HD],
                                             rpT[:, h % 2, q, :], start=False, stop=q == LT - 1)
                        last.then_inc(ret_v, 1)
                if h:
                    if h == 1:
                        pe.wait_ge(mix_ready, 1)
                    mix_turned(2 * h, 2 * h + 1)
                take(h % 3, ret_norm, h + 1)
                pe.wait_ge(ret_ot, h + 1)
                for t in range(LT):
                    last = pe.transpose(bank[h % 3][:, t * HD:(t + 1) * HD], ret_oT[0:HD, h % 2, t * P:(t + 1) * P],
                                        ident[0:HD, 0:HD])
                last.then_inc(ret_o, 1)
                pe.wait_ge(ret_p, (h + 1) * NT)
                pe.matmul(bank[h % 3][:, CT * HD:NT * HD], rctx[:, h, :],
                          r_v[:, CT, h * HD:(h + 1) * HD], start=True, stop=True).then_inc(ret_o, 1)
            pe.wait_ge(ret_kd, 2)
            take(7, ret_sto, 1)
            for r in range(2):
                for h in range(4):
                    last = pe.matmul(bank[7][0:HD, (4 * r + h) * HD:(4 * r + h + 1) * HD],
                                     kd[:, r, h * HD:(h + 1) * HD], r_v[:, CT, h * HD:(h + 1) * HD],
                                     start=True, stop=True)
            last.then_inc(ret_st, 1)

            pe.wait_ge(mix_ready, 4)
            mix_turned(0, 1)

            def back_product(n, k0, nk, src_h, src_l, last_operand=None):
                def group(i, j, half):
                    b = j % 2
                    wh, wl = slab(w_hi[b], nk, P), slab(w_lo[b], nk, P)
                    if half == 0:
                        pe.wait_ge(lo_ready, k0 + j + 1 if i is None else i + (k0 + j + 1))
                    cols = slice(half * HALF, (half + 1) * HALF)
                    for q in (MIX_ORDER if n == 0 else range(nk)):
                        if n == 0 and i is None and j == half == 0:
                            pe.wait_ge(h_ready, KD + MIX_ORDER.index(q) + 1)
                        if last_operand and i is None and j == half == 0 and q == nk - 1:
                            pe.wait_ge(*last_operand)
                        last = three(bank[2 * b + half][:, 0:HALF], wh[:, q, :], wl[:, q, :],
                                     src_h[:, q, cols], src_l[:, q, cols],
                                     q == (MIX_ORDER[0] if n == 0 else 0), q == (MIX_ORDER[-1] if n == 0 else nk - 1))
                    last.then_inc(back_done, 1)

                def turn_back(i, j):
                    ready, free = 2 * (n * KD + j + 1), n * KD + j + START
                    pe.wait_ge(back_ready, ready if i is None else i * 2 + ready)
                    pe.wait_ge(res_added, free if i is None else i + free)
                    for t in range(LT):
                        pe.transpose(bank[4][:, t * P:(t + 1) * P], back[:, j % 2, t * P:(t + 1) * P], ident)
                    pe.transpose(bank[5][:, 0:P], back[:, j % 2, LAT:TOK], ident).then_inc(back_turned, 1)

                group(None, 0, 0)
                group(None, 0, 1)
                with pe.Fori(0, KD // 2 - 1) as pair:
                    i = pair * 2
                    for j in (1, 2):
                        group(i, j, 0)
                        turn_back(i, j - 1)
                        group(i, j, 1)
                group(None, KD - 1, 0)
                if n == 2:
                    modulate(ADA_BESIDE[2] - 1, 0)
                    modulate(ADA_BESIDE[2] - 1, 1)
                turn_back(None, KD - 2)
                group(None, KD - 1, 1)
                if n == 2:
                    modulate(ADA_BESIDE[2] - 1, 2)
                    modulate(ADA_BESIDE[2] - 1, 3)
                turn_back(None, KD - 1)

            back_product(0, K_OUT, KD, h_hi, h_lo)
            pe.wait_ge(ln_hat, NT)
            to_features(2, x_tile)
            pe.wait_ge(h_ready, 3 * KD)
            first_ff = 0
            for part, nf in enumerate(FF_PARTS):
                k0 = K_FF[part]
                with pe.Fori(0, (nf) // 2) as pair:
                    i = pair * 2
                    for b in range(2):
                        wh = w_hi[b][:, 0:KD * 2 * P].rearrange("p (k u c) -> p k u c", k=KD, u=2)
                        wl = w_lo[b][:, 0:KD * 2 * P].rearrange("p (k u c) -> p k u c", k=KD, u=2)
                        pe.wait_ge(lo_ready, i + (k0 + b + 1))
                        f = first_ff + b
                        for u in range(2):
                            for half in range(2):
                                pe.wait_ge(silu_ready if u == 0 else act_ready, i * 2 + (2 * f + 1 + half))
                                for q in range(KD):
                                    cols = slice(half * HALF, (half + 1) * HALF)
                                    last = three(bank[2 * u + half][:, 0:HALF], wh[:, q, u, :], wl[:, q, u, :],
                                                 h_hi[:, q, cols], h_lo[:, q, cols], q == 0, q == KD - 1)
                                last.then_inc(gate_done if u == 0 else up_done, 1)
                                if half == 1:
                                    modulate(ADA_BESIDE[part], 2 * b + u, pair)
                first_ff += nf
                pe.wait_ge(silu_ready, 2 * first_ff + 1)
                pe.wait_ge(alo_ready, first_ff - 1)
                back_product(part + 1, K_DN[part], nf, a_hi, a_lo, (alo_ready, first_ff))

        @block.scalar
        def _(ac):
            def act(out, in_, func=ACT.Copy, **kw):
                return ac.activation(out, in_, func, **kw)

            def send(out, in_):
                ac.dma_start(out, in_).then_inc(out_sent, 16)

            ac.sem_inc(silu_ready, 2)
            def middle(n, shift, scale):
                for k in range(KD):
                    i, b = n * KD + k, k % 2
                    ac.wait_ge(fm_turned, i + 1)
                    if i >= 2:
                        ac.wait_ge(h_ready, i - 1)
                    act(hmid[:, b, 0:LAT], bank[4 + b], ACT.Identity,
                        scale=mod[:, scale + k, 0:1], bias=mod[:, shift + k, 0:1])
                    act(hmid[:, b, LAT:TOK], bank[6 + b][:, 0:P], ACT.Identity,
                        scale=mod[:, scale + k, 1:2], bias=mod[:, shift + k, 1:2]).then_inc(fm_mid, 1)
                    if n == 0 and k == 3:
                        split_hi(ac, 0)

            def to_h(*ks):
                for k in ks:
                    i = KD + MIX_ORDER.index(k)
                    ac.wait_ge(fm_turned, i + 1)
                    act(h_hi[:, k, :], ps[:, 3 * 512:3 * 512 + TOK]).then_inc(fm_mid, 1)

            def log_gamma():
                ac.wait_ge(params_in, 16 * PARAM_DMAS)
                act(dec[:, 0, :], decay[:], ACT.Exp).then_inc(ret_a, 1)
                ac.wait_ge(ret_d, 1)
                act(dec[:, 2, :], dec[:, 1, :], ACT.Ln).then_inc(ret_a, 1)

            ac.wait_ge(mod_ready, 1)
            middle(0, 0, KD)
            ac.wait_ge(x_spilled, 16)

            tok_out = {"z": None, "wq": w_qk[:, :, 0:256], "gq": g_qk[:, :, 0:256], "rv": r_v, "rg": r_g}

            def leave(k):
                name, _, tok = IN_SLABS[k]
                g = GROUPS_BEFORE[k]
                if tok:
                    for t in range(NT):
                        b = bank[g % 4]
                        ac.wait_ge(in_done, g + 1)
                        if name == "z":
                            act(z_act[:, t, :], b[:, 0:256], ACT.Silu)
                            last = act(dt_in[:, t * 8:(t + 1) * 8], b[:, 256:264])
                        elif name == "rg":
                            last = act(r_g[:, t, :], b[:, 0:256], ACT.Silu)
                        elif name in ("wkv", "gkv"):
                            qk, v = (w_qk, w_v) if name == "wkv" else (g_qk, g_v)
                            act(qk[:, t, 256:384], b[:, 0:P])
                            last = act(v[:, t, :], b[:, P:256])
                        else:
                            last = act(tok_out[name][:, t, :], b[:, 0:256])
                        last.then_inc(in_out, 1)
                        g += 1
                    return
                for m in range(2):
                    for half in range(2):
                        b = bank[g % 4]
                        ac.wait_ge(in_done, g + 1)
                        if name in ("rq", "rk"):
                            dst = (rqT if name == "rq" else rkT)[:, m, half * HALF:(half + 1) * HALF]
                            last = act(dst, b[:, 0:HALF])
                        else:
                            row = xbc_in[:, 2 * "xbc".index(name) + m, :]
                            if half == 0:
                                last = act(row[:, 1:1 + HALF], b[:, 0:HALF])
                            else:
                                act(row[:, 1 + HALF:1 + LAT], b[:, 0:LAT - HALF])
                                last = act(row[:, CON + 1:CON + 1 + P], b[:, LAT - HALF:HALF])
                        last.then_inc(in_out, 1)
                        g += 1

            for k in range(BEFORE_SSD):
                split_hi(ac, k + 1)
                leave(k)
                if k == 0:
                    log_gamma()
                if 1 <= k <= 3:
                    ac.wait_ge(pool_pads, 1)
                    ac.wait_ge(in_out, GROUPS_BEFORE[k])
                    for m in range(2 * k - 2, 2 * k):
                        act(xbc[:, m, 0:CON + P], xbc_in[:, m, 1:CON + P + 1], ACT.Identity,
                            scale=pcol[:, 48 + 6 + m:48 + 7 + m], bias=pcol[:, 66 + m:67 + m]).then_inc(conv_mid, 1)
                if k == 4:
                    for m in range(6):
                        ac.wait_ge(conv_acc, m + 1)
                        act(xbc[:, m, 0:CON + P], xbc[:, m, 0:CON + P], ACT.Silu).then_inc(conv_out, 1)
                if k == 3:
                    act(small[:, 9, 0:8], a_log[:], ACT.Exp)
                    ac.wait_ge(sp_d, 1)
                    act(small[:, 3, :], small[:, 2, :], ACT.Exp, scale=-1.0).then_inc(sp_a, 1)
                if k == 4:
                    ac.wait_ge(sp_d, 2)
                    act(small[:, 5, :], small[:, 4, :], ACT.Ln).then_inc(sp_a, 1)
            ac.wait_ge(decays_dve, 1)
            for n, i in enumerate((10, 11, 12)):
                act(small[:, 13 + n, :], small[:, i, :], ACT.Exp).then_inc(decays_act, 1)
            for n in range(2 * NT):
                ac.wait_ge(seg_done, n + 1)
                if n >= 1:
                    ac.wait_ge(pr_ready, n)
                act(seg, bank[1 + n % 2], ACT.Exp).then_inc(seg_exp, 1)
                if n == 0:
                    ac.wait_ge(st_ready, 14)
                    ac.dma_start(new_ssd[0, bass.ds(l, 1)].rearrange("l r (g h) p n -> (l h p) r g n", g=2),
                                 sst_out.rearrange("p (r g n) -> p r g n", r=2, g=2)).then_inc(sst_sent, 16)
            split_hi(ac, BEFORE_SSD + 1)
            leave(BEFORE_SSD)
            ac.wait_ge(ssd_gated, 1)
            act(small[:, 17, 0:NT], small[:, 16, 0:NT], ACT.Ln).then_inc(rms_act, 1)
            ac.wait_ge(rms_act, 1)
            act(small[:, 18, 0:NT], small[:, 17, 0:NT], ACT.Exp, scale=-0.5).then_inc(rms_act, 1)

            for k in range(BEFORE_SSD + 1, NIN):
                split_hi(ac, k + 1)
                if k == BEFORE_SSD + 2:
                    ac.wait_ge(mix_ready, 1)
                leave(k)
                if k == 9:
                    ac.wait_ge(g_rms, 1)
                    act(g_st[:, 1, :], g_st[:, 0, :], ACT.Ln).then_inc(g_rms, 1)
                    ac.wait_ge(g_rms, 2)
                    act(g_st[:, 2, :], g_st[:, 1, :], ACT.Exp, scale=-0.5).then_inc(g_rms, 1)

            for kind in range(2):
                def softmax(i):
                    t, h = items[i]
                    n, w = kind * NI + i, key_count("wg"[kind], t) * P
                    ac.wait_ge(nmax_ready, n + 1)
                    if n >= 2:
                        ac.wait_ge(pT_done, n - 1)
                    b0 = 1024 * (i % 2)
                    ac.activation(probs[:, i % 2, 0:w], ps[:, b0:b0 + w], ACT.Exp, scale=SCALE,
                                  bias=rowsum[:, 0, t, h:h + 1],
                                  accum_out=rowsum[:, 1, t, h:h + 1]).then_inc(probs_ready, 1)
                    if kind == 0 and h == 3:
                        ac.wait_ge(sink_sum, t + 1)
                        act(rowsum[:, 3, t, :], rowsum[:, 2, t, :], ACT.Exp).then_inc(sink_exp, 1)

                softmax(0)
                for i in range(NI):
                    if i + 1 < NI:
                        softmax(i + 1)
                    if has_b[kind][i]:
                        n = kind * NI + i
                        ac.wait_ge(pT_done, n + 1)
                        if n >= 2:
                            ac.wait_ge(o_done, n - 1)
                        act(pT[:, i % 2, 4, :], bank[5][:, 0:P]).then_inc(pTb_ready, 1)

            for i, (new, src) in enumerate(((new_swa_k, w_qk[:, CT, 256:384]), (new_swa_v, w_v[:, CT, :]),
                                            (new_gqa_k, g_qk[:, CT, 256:384]), (new_gqa_v, g_v[:, CT, :]))):
                send(new[0, bass.ds(l, 1)].rearrange("l s h d -> s (l h d)"), src)
            ac.wait_ge(o_out, 2 * NT)
            for r in range(2):
                for j in range(2):
                    lg = 8 + 2 * r + j
                    if r == 0:
                        act(rqd[:, r, j, :], k_("row"), ACT.Exp, scale=dec[:, 3, lg:lg + 1]).then_inc(ret_a, 1)
                    else:
                        act(rqd[:, r, j, :], k_("row"), ACT.Exp, scale=dec[:, 4, lg:lg + 1],
                            bias=dec513[:, j:j + 1]).then_inc(ret_a, 1)
            ac.wait_ge(ret_d, 3)
            act(kexp, kexp, ACT.Exp).then_inc(ret_a, 1)

            def head_out(h):
                ac.wait_ge(ret_v, h + 1)
                if h >= 2:
                    ac.wait_ge(ret_o, 2 * (h - 2) + 1)
                act(ret_oT[0:HD, h % 2, :], bank[7][0:HD, :]).then_inc(ret_ot, 1)

            for h in range(4):
                ac.wait_ge(ret_d, 4 + h)
                act(toep[:, h % 2, :], toep[:, h % 2, :], ACT.Exp).then_inc(ret_a, 1)
                if h:
                    head_out(h - 1)
                if h == 2:
                    to_h(2, 3)
            to_h(4, 5)
            head_out(3)
            to_h(6, 7)
            ac.wait_ge(ret_st, 1)
            act(rst_out[0:HD], bank[7][0:HD, :]).then_inc(ret_sto, 1)
            ac.wait_ge(ret_sto, 1)
            send(new_ret[0, bass.ds(l, 1)].rearrange("l r h d e -> d (l r h) e"),
                 rst_out[0:HD].rearrange("p (n e) -> p n e", n=8))
            ac.wait_ge(ret_d, 8)
            act(rstat[:, 2, :], rstat[:, 1, :], ACT.Ln).then_inc(ret_a, 1)
            ac.wait_ge(ret_a, 12)
            act(rstat[:, 3, :], rstat[:, 2, :], ACT.Exp, scale=-0.5).then_inc(ret_a, 1)

            to_h(0, 1)

            def come_back(n, k0, gate):
                def one(i, j, k):
                    if i is None:
                        if k + 1 < K_ALL:
                            split_hi(ac, k + 1)
                    else:
                        split_hi(ac, k + 1, i, back_done, 2 * (n * KD + j) + START)
                    b = j % 2
                    tile = mod[:, gate + j, :] if i is None else mod[:, bass.ds(i + (gate + j), 1), :]
                    act(gates[:, b:b + 1, :] if i is not None else gates[:, b, :], tile).then_inc(gates_ready, 1)
                    ready = n * KD + j + 1
                    ac.wait_ge(gates_ready, ready if i is None else i + ready)
                    for half in range(2):
                        need = 2 * (n * KD + j) + half + 1
                        ac.wait_ge(back_done, need + START if i is None else i * 2 + (need + START))
                        src = bank[2 * b + half]
                        if half == 0:
                            last = act(back[:, b, 0:HALF], src[:, 0:HALF], ACT.Copy, scale=gates[:, b, 0:1])
                        else:
                            act(back[:, b, HALF:LAT], src[:, 0:LAT - HALF], ACT.Copy, scale=gates[:, b, 0:1])
                            last = act(back[:, b, LAT:TOK], src[:, LAT - HALF:HALF], ACT.Copy, scale=gates[:, b, 1:2])
                        last.then_inc(back_ready, 1)

                slab_read(ac, k0 - 1)
                ac.wait_ge(mod_ready, 1 + KD // 2 if n == 0 else 2 + ADA_IN + ADA_GATE)
                with ac.Fori(0, (KD - 2) // 2) as pair:
                    i = pair * 2
                    for j in range(2):
                        one(i, j, k0 + j)
                for j in range(KD - 2, KD):
                    one(None, j, k0 + j)

            def inverse_sigma(n):
                ac.wait_ge(ln_d, 2 * n + 1)
                act(ln_r[:, 1, :], ln_r[:, 0, :], ACT.Ln).then_inc(ln_a, 1)
                ac.wait_ge(ln_a, 2 * n + 1)
                act(ln_r[:, 1, :], ln_r[:, 1, :], ACT.Exp, scale=-0.5).then_inc(ln_a, 1)

            come_back(0, K_OUT, 16)
            inverse_sigma(0)
            ac.wait_ge(ln_d, 2)
            for t in range(LN_DVE, NT):
                act(x[:, t, :], x[:, t, :], ACT.Identity, scale=ln_r[:, 1, t:t + 1], bias=ln_r[:, 2, t:t + 1]
                    ).then_inc(ln_hat, 1)
            ac.wait_ge(ln_folded, 1)
            middle(2, 24, 32)
            first_ff = 0
            for part, nf in enumerate(FF_PARTS):
                def one(i, j, k):
                    if i is None:
                        split_hi(ac, k + 1)
                    else:
                        split_hi(ac, k + 1, i, up_done, 2 * (first_ff + j) + START)
                    f, b = first_ff + j, j % 2

                    def at_(v):
                        return v if i is None else i * 2 + v
                    for half in range(2):
                        cols = slice(half * HALF, (half + 1) * HALF)
                        ac.wait_ge(gate_done, at_(2 * f + half + 1))
                        act(sg[:, b, cols], bank[half][:, 0:HALF], ACT.Silu).then_inc(silu_ready, 1)

                slab_read(ac, K_FF[part] - 1)
                with ac.Fori(0, (nf - 2) // 2) as pair:
                    i = pair * 2
                    for j in range(2):
                        one(i, j, K_FF[part] + j)
                for j in range(nf - 2, nf):
                    one(None, j, K_FF[part] + j)
                first_ff += nf
                come_back(part + 1, K_DN[part], 40)
            inverse_sigma(1)
            ac.wait_ge(ln_a, 4)
            for n, t in enumerate(LN_ORDER[:2]):
                ac.wait_ge(ln_centred, n + 1)
                act(x[:, t, :], x[:, t, :], ACT.Copy, scale=ln_r[:, 1, t:t + 1]).then_inc(ln_a, 1)
            ac.wait_ge(out_sent, 16 * SENDS)
            ac.wait_ge(sst_sent, 16)

        @block.vector
        def _(ve):
            steps = [0]

            def step(ins):
                steps[0] += 1
                ins.then_inc(dve_step, 1)
                ve.wait_ge(dve_step, steps[0])

            def tt(out, a, b, op=ALU.mult):
                return ve.tensor_tensor(out, a, b, op)

            def ts(out, a, s1, s2, op0, op1=ALU.bypass):
                return ve.tensor_scalar(out, a, s1, s2, op0, op1)

            def wide(ap, n):
                return ap.unsqueeze(len(ap.shape)).to_broadcast(list(ap.shape) + [n])

            ve.sem_inc(res_added, START)
            ve.sem_inc(act_ready, 2)
            ve.wait_ge(params_turned, 1)
            ve.tensor_copy(pcol[:], bank[3][:, 0:88]).then_inc(params_ready, 1)
            ve.wait_ge(params_ready, 1)
            ts(pcol[:, 8:16], pcol[:, 8:16], 1.0, None, ALU.add)
            step(ts(pcol[:, 32:40], pcol[:, 32:40], 1.0, None, ALU.add))
            tt(mod[:, 0:16, :], mod_next, wide(pcol[:, 0:16], 2), ALU.add).then_inc(mod_ready, 1)

            def split_h(n):
                for k in range(KD):
                    i, b = n * KD + k, k % 2
                    ve.wait_ge(fm_mid, i + 1)
                    step(ve.tensor_copy(h_hi[:, k, :], hmid[:, b, :]))
                    tt(h_lo[:, k, :], hmid[:, b, :], h_hi[:, k, :].bitcast(F32), ALU.subtract).then_inc(h_ready, 1)
                    if n == 0 and k == 4:
                        split_lo(ve, 0)

            def low_part(*ks):
                for k in ks:
                    ve.wait_ge(fm_mid, KD + MIX_ORDER.index(k) + 1)
                    tt(h_lo[:, k, :], ps[:, 3 * 512:3 * 512 + TOK], h_hi[:, k, :].bitcast(F32), ALU.subtract
                       ).then_inc(h_ready, 1)

            split_h(0)
            ve.wait_ge(x_spilled, 16)

            def log_gamma():
                ve.wait_ge(ret_a, 1)
                ts(dec[:, 1, :], dec[:, 0, :], -1.0, 1.0, ALU.mult, ALU.add).then_inc(ret_d, 1)
                ve.wait_ge(ret_d, 1)
                step(ts(dec[:, 3, :], dec[:, 1, :], -1.0, None, ALU.add))
                step(tt(dec[:, 3, :], dec[:, 3, :], dec[:, 0, :], ALU.add))
                step(ve.reciprocal(dec[:, 4, :], dec[:, 1, :]))
                step(tt(dec[:, 3, :], dec[:, 3, :], dec[:, 4, :]))
                ve.wait_ge(ret_a, 2)
                step(tt(dec[:, 3, :], dec[:, 2, :], dec[:, 3, :], ALU.subtract))
                ts(dec[:, 4, :], dec[:, 3, :], -1.0, None, ALU.mult)
                ts(dec513[:], dec[:, 3, 10:12], LAT + 1.0, None, ALU.mult)
                ts(nsink[:], sink[:], -1.0, None, ALU.mult).then_inc(ret_d, 1)

            def modulated(a):
                m = 2 * KD + 2 * a
                ve.wait_ge(ada_used, a + 1)
                tt(mod[:, m:m + 2, :], bank[6][:, 0:4].rearrange("p (m c) -> p m c", c=2),
                   wide(pcol[:, m:m + 2], 2), ALU.add).then_inc(mod_ready, 1)
            z, az, t_, u, ln_u = (small[:, i, :] for i in (1, 2, 3, 4, 5))
            for k in range(BEFORE_SSD):
                if k > 0:
                    modulated(k - 1)
                split_lo(ve, k + 1)
                if k == 0:
                    log_gamma()
                if 1 <= k <= 3:
                    ve.wait_ge(pool_pads, 1)
                    for m in range(2 * k - 2, 2 * k):
                        ve.wait_ge(conv_mid, m + 1)
                        acc = xbc[:, m, 0:CON + P]
                        step(ve.scalar_tensor_tensor(acc, xbc_in[:, m, 0:CON + P], pcol[:, 48 + m:49 + m], acc,
                                                     ALU.mult, ALU.add))
                        ve.scalar_tensor_tensor(acc, xbc_in[:, m, 2:CON + P + 2], pcol[:, 60 + m:61 + m], acc,
                                                ALU.mult, ALU.add).then_inc(conv_acc, 1)
                if k == 3:
                    ve.wait_ge(in_out, GROUPS_BEFORE[4])
                    step(tt(z.rearrange("p (t c) -> p t c", c=8), dt_in.rearrange("p (t c) -> p t c", c=8),
                            dt_bias[:].unsqueeze(1).to_broadcast([P, NT, 8]), ALU.add))
                    ve.scalar_tensor_tensor(az, z, -1.0, z, ALU.mult, ALU.max).then_inc(sp_d, 1)
                if k == 4:
                    ve.wait_ge(sp_a, 1)
                    ts(u, t_, 1.0, None, ALU.add).then_inc(sp_d, 1)
                    ve.wait_ge(sp_d, 2)
                if k == 5:
                    step(ts(small[:, 6, :], u, -1.0, None, ALU.add))
                    step(tt(small[:, 6, :], t_, small[:, 6, :], ALU.subtract))
                    step(ve.reciprocal(small[:, 7, :], u))
                    step(tt(small[:, 6, :], small[:, 6, :], small[:, 7, :]))
                    ve.wait_ge(sp_a, 2)
                    step(tt(small[:, 6, :], ln_u, small[:, 6, :], ALU.add))
                    step(ve.scalar_tensor_tensor(small[:, 8, :], z, 0.0, small[:, 6, :], ALU.max, ALU.add))
                    ve.scalar_tensor_tensor(small[:, 0, :].rearrange("p (t c) -> p t c", c=8),
                                            small[:, 8, :].rearrange("p (t c) -> p t c", c=8), -1.0,
                                            small[:, 9, 0:8].unsqueeze(1).to_broadcast([P, NT, 8]),
                                            ALU.mult, ALU.mult).then_inc(dt_ready, 1)

            modulated(BEFORE_SSD - 1)
            for m in range(4):
                ve.wait_ge(ssd_turned, m + 1)
                ve.tensor_copy(xb[:, 0:LT, m * P:(m + 1) * P],
                               bank[4 + m].rearrange("p (t c) -> p t c", t=LT)).then_inc(st_ready, 1)
            ve.wait_ge(ssd_turned, 5)
            ve.tensor_copy(xb[:, CT, :], bank[4]).then_inc(st_ready, 1)
            ve.wait_ge(ssd_turned, 6)
            ve.tensor_copy(hst[:, 0, 0, :], bank[5][:, 0:256])
            ve.tensor_copy(hst[:, 1, 3, :], bank[5][:, 256:512]).then_inc(st_ready, 1)
            ve.wait_ge(st_ready, 6)
            ve.wait_ge(cum_done, 1)

            def eight(ap):
                return ap.rearrange("p (t r h) -> p t r h", t=NT, r=2)
            ve.tensor_copy(eight(small[:, 10, :])[:, :, 0, :], eight(bank[6][:, 0:40])[:, :, 0, :])
            ve.tensor_copy(eight(small[:, 10, :])[:, :, 1, :], eight(bank[6][:, 40:80])[:, :, 1, :])
            step(ve.tensor_copy(small[:, 11, :], bank[6][:, 80:120]))
            tt(small[:, 12, :], small[:, 11, :], small[:, 10, :], ALU.subtract).then_inc(decays_dve, 1)
            ve.wait_ge(decays_act, 3)

            def heads(ap):
                return ap.rearrange("p (h d) -> p h d", d=HD)
            n = 0
            for r in range(2):
                for t in ([0, 1, 2] if r == 0 else [3, 2, 1]):
                    n += 1
                    to = t + 1 if r == 0 else t - 1
                    decayed = small[:, 14, t * 8 + r * 4:t * 8 + r * 4 + 4]
                    step(tt(heads(hst[:, r, to, :]), heads(hst[:, r, t, :]), wide(decayed, HD)))
                    ve.wait_ge(upd_done, n)
                    tt(hst[:, r, to, :], hst[:, r, to, :], bank[4 + n % 2][:, 0:256], ALU.add).then_inc(st_ready, 1)
                    ve.wait_ge(st_ready, 6 + n)
                n += 1
                ve.wait_ge(upd_done, n)
                ve.tensor_copy(sst_out[:, r * 256:(r + 1) * 256], bank[6 + r][:, 0:256]).then_inc(st_ready, 1)

            for t in range(NT):
                ve.wait_ge(sc_done, t + 1)
                for r, mask in ((0, upper), (1, lower)):
                    tt(sm[:, r, :].rearrange("p (g q) -> p g q", g=2),
                       bank[0][:, 0:256].rearrange("p (g q) -> p g q", g=2),
                       mask.unsqueeze(1).to_broadcast([P, 2, P])).then_inc(sm_ready, 1)
                for r in range(2):
                    ve.wait_ge(sm_ready, 2 * t + r + 1)
                    ve.wait_ge(seg_exp, 2 * t + r + 1)
                    if t > 0:
                        ve.wait_ge(y_done, t)
                    tt(pr[:, r, :].rearrange("p (g h q) -> p g h q", g=2, h=2),
                       seg.rearrange("p (g h q) -> p g h q", g=2, h=2),
                       sm[:, r, :].rearrange("p (g q) -> p g q", g=2).unsqueeze(2).to_broadcast([P, 2, 2, P])
                       ).then_inc(pr_ready, 1)
                ve.wait_ge(y_done, t + 1)
                if t == 0:
                    ve.wait_ge(sst_sent, 16)
                yb = bank[4 + t % 2][:, 0:256]
                if t < CT:
                    step(tt(yi.rearrange("p (g d) -> p g d", d=HD), bank[3].rearrange("p (g d) -> p g d", d=HD),
                            wide(small[:, 13, t * 8:(t + 1) * 8], HD)))
                    step(tt(mix_s[:, t, :], yb, yi[:, 0:256], ALU.add))
                    tt(mix_s[:, t, :], mix_s[:, t, :], yi[:, 256:512], ALU.add).then_inc(y_out, 1)
                else:
                    ve.tensor_copy(mix_s[:, t, :], yb).then_inc(y_out, 1)
                    ve.wait_ge(y_out, NT)
            split_lo(ve, BEFORE_SSD + 1)
            ve.wait_ge(skip_ready, 1)
            step(tt(mix_s, mix_s, xdt[:, 0], ALU.add))
            step(tt(mix_s, mix_s, z_act))
            step(tt(ssq, mix_s, mix_s))
            step(ve.tensor_reduce(small[:, 16, 0:NT], ssq, AX, ALU.add))
            ts(small[:, 16, 0:NT], small[:, 16, 0:NT], 1.0 / 256, 1e-6, ALU.mult, ALU.add).then_inc(ssd_gated, 1)
            modulated(BEFORE_SSD)
            ve.wait_ge(rms_act, 2)
            step(tt(mix_s, mix_s, wide(small[:, 18, 0:NT], 256)))
            tt(mix_s, mix_s, norm_g[:].unsqueeze(1).to_broadcast([P, NT, 256])).then_inc(mix_ready, 1)

            for k in range(BEFORE_SSD + 1, NIN):
                if k > BEFORE_SSD + 1:
                    modulated(k - 1)
                split_lo(ve, k + 1)
                if k == 8:
                    ve.wait_ge(in_out, GROUPS_BEFORE[8])
                    flat = g_qk.rearrange("p t c -> p (t c)").rearrange("p (n d) -> p n d", d=HD)
                    step(tt(gsq, g_qk, g_qk))
                    step(ve.tensor_reduce(g_st[:, 0, :], gsq.rearrange("p t c -> p (t c)").rearrange(
                        "p (n d) -> p n d", d=HD), AX, ALU.add))
                    ts(g_st[:, 0, :], g_st[:, 0, :], 1.0 / HD, 1e-6, ALU.mult, ALU.add).then_inc(g_rms, 1)
                if k == 10:
                    ve.wait_ge(g_rms, 3)
                    step(tt(flat, flat, wide(g_st[:, 2, :], HD)))
                    tt(g_qk, g_qk, qk_gain[:].unsqueeze(1).to_broadcast([P, NT, 384])).then_inc(g_normed, 1)
            modulated(NIN - 1)
            gain, bias = pcol[:, 72:80], pcol[:, 80:88]
            ve.wait_ge(mod_ready, 1 + ADA_IN)
            fold = ln_fold[:].rearrange("p (m c) -> p m c", c=2)
            step(tt(fold, mod[:, 4 * KD:5 * KD, :], wide(bias, 2)))
            tt(mod[:, 3 * KD:4 * KD, :], mod[:, 3 * KD:4 * KD, :], fold, ALU.add)
            tt(mod[:, 4 * KD:5 * KD, :], mod[:, 4 * KD:5 * KD, :], wide(gain, 2)).then_inc(ln_folded, 1)

            for kind in range(2):
                for j in range(3):
                    ve.wait_ge(qk_turned, 4 * kind + j + 1)
                    ve.tensor_copy(qkT[:, j, 0:LAT], bank[4 + j]).then_inc(qk_ready, 1)
                ve.wait_ge(qk_turned, 4 * kind + 4)
                ve.tensor_copy(qkT[:, :, LAT:TOK], bank[7][:, 0:3 * P].rearrange("p (j t) -> p j t", j=3))
                ve.tensor_copy(qkT[:, 2, TOK:TOK + P], bank[7][:, 3 * P:4 * P]).then_inc(qk_ready, 1)
                mix = (mix_w, mix_g)[kind]

                def neg_max(i):
                    t, h = items[i]
                    n, w = kind * NI + i, key_count("wg"[kind], t) * P
                    ve.wait_ge(s_done, n + 1)
                    b0 = 1024 * (i % 2)
                    nm = rowsum[:, 0, t, h:h + 1]
                    step(ve.tensor_reduce(rowsum[:, 4, t, h:h + 1], ps[:, b0:b0 + w], AX, ALU.max))
                    if kind == 0:
                        ts(nm, rowsum[:, 4, t, h:h + 1], -SCALE, nsink[:, h:h + 1], ALU.mult, ALU.min
                           ).then_inc(nmax_ready, 1)
                        if h == 3:
                            ve.wait_ge(nmax_ready, n + 1)
                            tt(rowsum[:, 2, t, :], rowsum[:, 0, t, :], sink[:], ALU.add).then_inc(sink_sum, 1)
                    else:
                        ts(nm, rowsum[:, 4, t, h:h + 1], -SCALE, None, ALU.mult).then_inc(nmax_ready, 1)

                def finish(t):
                    ve.wait_ge(o_done, kind * NI + 4 * (t + 1))
                    if kind == 0:
                        ve.wait_ge(sink_exp, t + 1)
                        step(tt(rowsum[:, 1, t, :], rowsum[:, 1, t, :], rowsum[:, 3, t, :], ALU.add))
                    step(ve.reciprocal(rowsum[:, 1, t, :], rowsum[:, 1, t, :]))
                    tt(heads(mix[:, t, :]), heads(bank[6 + t % 2][:, 0:256]), wide(rowsum[:, 1, t, :], HD)
                       ).then_inc(o_out, 1)

                neg_max(0)
                neg_max(1)
                for i in range(NI):
                    n, w = kind * NI + i, min(key_count("wg"[kind], items[i][0]), 4)
                    ve.wait_ge(pT_done, n + 1)
                    if n >= 2:
                        ve.wait_ge(o_done, n - 1)
                    ve.tensor_copy(pT[:, i % 2, 0:w, :], bank[4][:, 0:w * P].rearrange("p (k q) -> p k q", k=w)
                                   ).then_inc(pTa_ready, 1)
                    if i + 2 < NI:
                        neg_max(i + 2)
                    if i % 4 == 0 and i > 0:
                        finish(i // 4 - 1)
                finish(NT - 1)
            ve.wait_ge(o_out, 2 * NT)

            ve.wait_ge(out_sent, 64)
            tt(kexp, k_("kpos"), dec[:, 3, 0:8]).then_inc(ret_d, 1)
            ve.wait_ge(ret_a, 7)
            ve.wait_ge(ret_k, 1)
            for r in range(2):
                ve.scalar_tensor_tensor(heads(kd[:, r, :]), heads(bank[4][:, 0:256]), SCALE,
                                        wide(kexp[:, 4 * r:4 * r + 4], HD), ALU.mult, ALU.mult).then_inc(ret_kd, 1)
            def distances(h):
                at_ = toep[:, h % 2, :]
                if h:
                    ve.wait_ge(ret_a, 7 + h)
                ts(at_, k_("dist"), 0.0, dec[:, 3, h:h + 1], ALU.max, ALU.mult)
                step(ts(toep_b, k_("dist"), 0.0, dec[:, 3, 4 + h:5 + h], ALU.min, ALU.mult))
                tt(at_, at_, toep_b, ALU.subtract).then_inc(ret_d, 1)

            def centre(h):
                o, src = r_o[:, :, h * HD:(h + 1) * HD], bank[h % 3][:, 0:NT * HD].rearrange("p (t d) -> p t d", t=NT)
                mean, var = rstat[:, 0, h * NT:(h + 1) * NT], rstat[:, 1, h * NT:(h + 1) * NT]
                ve.wait_ge(ret_o, 2 * (h + 1))
                ve.tensor_copy(o, src).then_inc(ret_norm, 1)
                ve.wait_ge(ret_norm, h + 1)
                step(ve.tensor_reduce(mean, o, AX, ALU.add))
                step(ts(mean, mean, 1.0 / HD, None, ALU.mult))
                step(tt(o, o, wide(mean, HD), ALU.subtract))
                step(tt(rsq, o, o))
                step(ve.tensor_reduce(var, rsq, AX, ALU.add))

            distances(0)
            for h in range(4):
                if h:
                    ve.wait_ge(ret_p, h * NT)
                gamma = toep[:, h % 2, :]
                ve.wait_ge(ret_a, 8 + h)
                step(tt(gamma[:, 3 * P:4 * P], gamma[:, 3 * P:4 * P], ident, ALU.add))
                for kt in range(NT):
                    n = h * NT + kt + 1
                    ve.wait_ge(ret_s, n)
                    if h >= 2 and kt == 0:
                        ve.wait_ge(ret_o, 2 * (h - 1))
                    src = bank[5 + n % 2]
                    if kt < CT:
                        ve.scalar_tensor_tensor(rpT[:, h % 2, kt, :], src, SCALE,
                                                gamma[:, 3 * P - kt * P:3 * P - kt * P + LAT],
                                                ALU.mult, ALU.mult).then_inc(ret_p, 1)
                    else:
                        ve.scalar_tensor_tensor(rctx[:, h, :], src[:, 0:P], SCALE, gamma[:, 3 * P:4 * P],
                                                ALU.mult, ALU.mult).then_inc(ret_p, 1)
                    if kt == 1 and h < 3:
                        distances(h + 1)
                    if kt == 3 and h:
                        centre(h - 1)
                if h:
                    low_part(2 * h, 2 * h + 1)
            centre(3)
            ts(rstat[:, 1, :], rstat[:, 1, :], 1.0 / HD, 1e-5, ALU.mult, ALU.add).then_inc(ret_d, 1)
            ve.wait_ge(ret_a, 13)
            step(tt(r_o.rearrange("p t (h d) -> p t h d", h=4), r_o.rearrange("p t (h d) -> p t h d", h=4),
                    wide(rstat[:, 3, :].rearrange("p (h t) -> p t h", h=4), HD)))
            ve.wait_ge(ret_gate, 1)
            tt(mix_r, r_o, r_g).then_inc(mix_ready, 3)

            low_part(0, 1)

            def add_back(n, k0, alpha):
                def one(i, j, k):
                    if i is not None or k + 1 < K_ALL:
                        split_lo(ve, k + 1, i)
                    if n in (0, len(FF_PARTS)) and i is None:
                        for quarter in ((0, 1), (2,))[j - (KD - 2)]:
                            ve.wait_ge(res_added, n * KD + 2 * quarter + 2 + START)
                            statistics(quarter)
                    if n == 0:
                        ve.wait_ge(x_back, 16)
                    need = n * KD + j + 1
                    ve.wait_ge(back_turned, need if i is None else i + need)
                    at_ = slice(j * P, (j + 1) * P) if i is None else bass.ds(i * P + j * P, P)
                    lat, con = x[:, 0:LT, at_], x[:, CT, at_]
                    ve.scalar_tensor_tensor(lat, lat, alpha, bank[4].rearrange("p (t c) -> p t c", t=LT),
                                            ALU.mult, ALU.add)
                    ve.scalar_tensor_tensor(con, con, alpha, bank[5][:, 0:P], ALU.mult, ALU.add).then_inc(res_added, 1)

                with ve.Fori(0, (KD - 2) // 2) as pair:
                    i = pair * 2
                    for j in range(2):
                        one(i, j, k0 + j)
                for j in range(KD - 2, KD):
                    one(None, j, k0 + j)

            QUARTER = DM // 4

            def statistics(q):
                for t in range(NT):
                    last = ve.bn_stats(ln_st[:, t, 6 * q:6 * q + 6], x[:, t, QUARTER * q:QUARTER * (q + 1)])
                return last

            def moments(n, added):
                ve.wait_ge(res_added, added + START)
                step(statistics(3))
                for t in range(NT):
                    last = ve.bn_aggr(ln_mv[:, t, :], ln_st[:, t, :])
                step(last)
                ts(ln_r[:, 0, :], ln_mv[:, :, 1], 1e-5, None, ALU.add).then_inc(ln_d, 1)

            add_back(0, K_OUT, ALPHA)
            moments(0, KD)
            ve.wait_ge(ln_a, 2)
            ve.scalar_tensor_tensor(ln_r[:, 2, :], ln_mv[:, :, 0], -1.0, ln_r[:, 1, :], ALU.mult, ALU.mult
                                    ).then_inc(ln_d, 1)
            for t in range(LN_DVE):
                ts(x[:, t, :], x[:, t, :], ln_mv[:, t, 0:1], ln_r[:, 1, t:t + 1], ALU.subtract, ALU.mult
                   ).then_inc(ln_hat, 1)
            split_h(2)
            ve.wait_ge(out_sent, 16 * SENDS)
            first_ff = 0
            for part, nf in enumerate(FF_PARTS):
                def one(i, j, k):
                    split_lo(ve, k + 1, i)
                    f, b = first_ff + j, j % 2

                    def at_(v):
                        return v if i is None else i * 2 + v
                    for half in range(2):
                        cols = slice(half * HALF, (half + 1) * HALF)
                        ve.wait_ge(silu_ready, at_(2 * f + half + 3))
                        ve.wait_ge(up_done, at_(2 * f + half + 1 + START))
                        tt(act_[:, b, cols], sg[:, b, cols], bank[2 + half][:, 0:HALF]).then_inc(act_ready, 1)
                    ve.wait_ge(act_ready, at_(2 * f + 4))
                    hi, lo = ((a[:, j, :] if i is None else a[:, bass.ds(i + j, 1), :].rearrange("p o t -> p (o t)"))
                              for a in (a_hi, a_lo))
                    ts(hi, act_[:, b, :], 1.0, None, ALU.mult).then_inc(ahi_ready, 1)
                    ve.wait_ge(ahi_ready, f + 1 if i is None else i + (f + 1))
                    tt(lo, act_[:, b, :], hi.bitcast(F32), ALU.subtract).then_inc(alo_ready, 1)

                def modulated(pair, m):
                    used = ADA_BESIDE[part] + 1
                    ve.wait_ge(ada_used, pair + used if m is None else m // 2 + used)
                    col = bass.ds(pair * 2, 2) if m is None else slice(m, m + 2)
                    dst = mod[:, 5 * KD:6 * KD, :] if part == 0 else mod_next[:, (0, 0, KD + 2)[part]:2 * KD, :]
                    ts(dst[:, col, :], bank[6][:, 0:4].rearrange("p (m c) -> p m c", c=2), 1.0, None, ALU.mult
                       ).then_inc(mod_ready, 1)

                with ve.Fori(0, (nf - 2) // 2) as pair:
                    i = pair * 2
                    for j in range(2):
                        one(i, j, K_FF[part] + j)
                    modulated(pair, None)
                for j in range(nf - 2, nf):
                    one(None, j, K_FF[part] + j)
                modulated(None, nf - 2)
                if part == 0:
                    ve.wait_ge(mod_ready, 1 + ADA_IN + ADA_GATE)
                    tt(mod[:, 5 * KD:6 * KD, :], mod[:, 5 * KD:6 * KD, :], wide(pcol[:, 5 * KD:6 * KD], 2), ALU.add
                       ).then_inc(mod_ready, 1)
                first_ff += nf
                if part == 0:
                    ve.wait_ge(ln_out, NT)
                add_back(part + 1, K_DN[part], ALPHA if part == 0 else 1.0)
                if part == 1:
                    ve.wait_ge(ada_used, ADA_BESIDE[2])
                    ve.tensor_copy(mod_next[:, KD:KD + 2, :], bank[6][:, 0:4].rearrange(
                        "p (m c) -> p m c", c=2)).then_inc(mod_ready, 1)
            moments(1, KD * (1 + len(FF_PARTS)))
            ve.wait_ge(ln_in[1], 32)
            for t in LN_ORDER:
                ve.scalar_tensor_tensor(x[:, t, :], x[:, t, :], ln_mv[:, t, 0:1], ln_gb[:, 0, :],
                                        ALU.subtract, ALU.mult).then_inc(ln_centred, 1)
            ve.wait_ge(ln_a, 4)
            ve.wait_ge(ln_centred, NT)
            for t in LN_ORDER[2:]:
                ve.scalar_tensor_tensor(x[:, t, :], x[:, t, :], ln_r[:, 1, t:t + 1], ln_gb[:, 1, :],
                                        ALU.mult, ALU.add).then_inc(ln_out, 1)
            ve.wait_ge(ln_out, 2 * NT)

        @block.gpsimd
        def _(po):
            steps = [0]

            def step(ins):
                steps[0] += 1
                ins.then_inc(pool_step, 1)
                po.wait_ge(pool_step, steps[0])

            def tt(out, a, b, op=ALU.mult):
                return po.tensor_tensor(out, a, b, op)

            def wide(ap, n):
                return ap.unsqueeze(len(ap.shape)).to_broadcast(list(ap.shape) + [n])

            for a in (0, LAT + 1, LAT + 2, PAD - 1):
                last = po.memset(xbc_in[:, :, a:a + 1], 0.0)
            last.then_inc(pool_pads, 1)
            po.wait_ge(dt_ready, 1)
            po.wait_ge(conv_acc, 6)
            po.wait_ge(st_ready, 5)
            dt8 = small[:, 8, :].rearrange("p (t c) -> p t c", t=NT)
            x_part = xb[:, :, 0:256].rearrange("p t (h d) -> p t h d", d=HD)
            for r in range(2):
                tt(xdt[:, r].rearrange("p t (h d) -> p t h d", d=HD), x_part,
                   wide(dt8[:, :, 4 * r:4 * r + 4], HD)).then_inc(xdt_ready, 1)
            po.wait_ge(decays_act, 3)
            to_end = small[:, 15, :].rearrange("p (t c) -> p t c", t=NT)
            for r in range(2):
                po.wait_ge(xdt_ready, r + 1)
                if r:
                    po.wait_ge(upd_done, 4)
                tt(xw.rearrange("p t (h d) -> p t h d", d=HD), xdt[:, r].rearrange("p t (h d) -> p t h d", d=HD),
                   wide(to_end[:, :, 4 * r:4 * r + 4], HD)).then_inc(xw_ready, 1)
            n = 0
            for t in range(NT):
                for r, mask in ((0, k_("slower")), (1, k_("supper"))):
                    n += 1
                    if n > 2:
                        po.wait_ge(seg_done, n - 2)
                    tt(dam[:, r, :].rearrange("p (h q) -> p h q", h=4), mask.unsqueeze(1).to_broadcast([P, 4, P]),
                       wide(small[:, 0, t * 8 + r * 4:t * 8 + r * 4 + 4], P)).then_inc(dam_ready, 1)
            po.wait_ge(y_done, NT)
            tt(xdt[:, 0].rearrange("p t (h d) -> p t h d", d=HD), x_part,
               wide(skip_d[:].unsqueeze(1).to_broadcast([P, NT, 4]), HD)).then_inc(skip_ready, 1)

            def rope(kind, qk, out):
                for t in range(NT):
                    if t or kind:
                        po.wait_ge(roped, kind * NT + t)
                    q_in = qk[:, t, 0:256].rearrange("p (g j d) -> p g j d", g=2, j=2)
                    q_out = out[:, t, 0:256].rearrange("p (j g d) -> p g j d", g=2, j=2)
                    if t == CT:
                        po.tensor_copy(q_out, q_in)
                        po.tensor_copy(out[:, t, 256:384], qk[:, t, 256:384]).then_inc(roped, 1)
                        continue
                    cos = k_("cos")[:, t * HD:(t + 1) * HD]
                    sin = k_("sin")[:, t * HD:(t + 1) * HD].rearrange("p (f s d) -> p f s d", f=2, s=2)
                    xin = qk[:, t, :].rearrange("p (h f s d) -> p h f s d", h=6, f=2, s=2)
                    rot = rope_a.rearrange("p (h f s d) -> p h f s d", h=6, f=2, s=2)
                    for s in range(2):
                        tt(rot[:, :, :, s, :], xin[:, :, :, 1 - s, :],
                           sin[:, :, s, :].unsqueeze(1).to_broadcast([P, 6, 2, HD // 4]))
                    step(tt(rope_b.rearrange("p (h d) -> p h d", h=6), qk[:, t, :].rearrange("p (h d) -> p h d", h=6),
                            cos.unsqueeze(1).to_broadcast([P, 6, HD])))
                    ra = rope_a[:, 0:256].rearrange("p (g j d) -> p g j d", g=2, j=2)
                    rb = rope_b[:, 0:256].rearrange("p (g j d) -> p g j d", g=2, j=2)
                    tt(q_out, ra, rb, ALU.add)
                    tt(out[:, t, 256:384], rope_a[:, 256:384], rope_b[:, 256:384], ALU.add).then_inc(roped, 1)

            po.wait_ge(mix_ready, 1)
            po.wait_ge(in_out, GROUPS_BEFORE[BEFORE_SSD])
            rope(0, w_qk, qkr)
            po.wait_ge(in_out, GROUPS_BEFORE[NIN])
            tt(r_g, r_g, gn_g[:].unsqueeze(1).to_broadcast([P, NT, 256])).then_inc(ret_gate, 1)
            po.wait_ge(g_normed, 1)
            po.wait_ge(qk_turned, 4)
            rope(1, g_qk, qkr)
            for n in range(4):
                po.wait_ge(ret_a, 3 + n)
                r, j = n // 2, n % 2
                tt(rqd[:, r, j, :], rqd[:, r, j, :], rqT[:, j, 0:LAT]).then_inc(ret_qd, 1)
            po.wait_ge(ln_in[0], 32)
            po.wait_ge(fm_turned, 3 * KD)
            for t in range(NT):
                step(tt(x[:, t, :], x[:, t, :], ln_gb[:, 0, :]))
                tt(x[:, t, :], x[:, t, :], ln_gb[:, 1, :], ALU.add).then_inc(ln_out, 1)
            for n, t in enumerate(LN_ORDER[:2]):
                po.wait_ge(ln_a, 5 + n)
                tt(x[:, t, :], x[:, t, :], ln_gb[:, 1, :], ALU.add).then_inc(ln_out, 1)
    layer_loop.__exit__(None, None, None)

    nc.all_engine_barrier(sems_to_clear=range(numbers[0], numbers[-1] + 1))
    with nc.Block() as block:
        @block.sync
        def _(sp):
            sp.dma_start(y_sample[0].rearrange("(t p) d -> p t d", p=P), x[:, 0:LT, :]).then_inc(y_sent, 16)
            sp.dma_start(y_prompt[0], x[:, CT, :]).then_inc(y_sent, 16)
            sp.wait_ge(y_sent, 32)
    ctx.close()


_INS = ["x_prompt", "x_sample", "cache_gqa_k", "cache_gqa_v", "cache_swa_k", "cache_swa_v", "state_ret", "state_ssd",
        "c", "c_ctx", "ada_w", "ada_b", "w_in", "ret_decay", "ret_gn_g", "gqa_q_norm", "gqa_k_norm", "ssd_conv_w",
        "ssd_conv_b", "ssd_dt_bias", "ssd_a_log", "ssd_d", "ssd_norm_g", "swa_sink", "w_out", "ln1_g", "ln1_b",
        "w_ffn_in", "w_ffn_out", "ln2_g", "ln2_b"]
_OUTS = [(1, CTX, DM), (1, LAT, DM)] + [(1, DEPTH, CTX, 2, HD)] * 4 + [(1, DEPTH, 2, 4, HD, HD),
                                                                       (1, DEPTH, 2, 4, HD, P)]


def kernel(**inputs):
    import concourse.bacc as bacc
    from concourse.bass_utils import run_bass_kernel_spmd

    nc = bacc.Bacc("TRN2", target_bir_lowering=False, num_devices=1)
    arrays = {f"in_{name}": np.ascontiguousarray(inputs[name]) for name in _INS}
    arrays["in_consts"] = constants()
    args = [nc.dram_tensor(name, a.shape, F32, kind="ExternalInput").ap() for name, a in arrays.items()]
    args += [nc.dram_tensor(f"out_{i}", shape, F32, kind="ExternalOutput").ap() for i, shape in enumerate(_OUTS)]
    build(nc, *args)
    r = run_bass_kernel_spmd(nc, [arrays], core_ids=[0])
    return tuple(r.results[0][f"out_{i}"] for i in range(len(_OUTS)))
```
